# Optimizing a Trainium2 kernel written in Bass

```python
import numpy as np
import jax
import jax.numpy as jnp
from jax import lax

D_MODEL = 2048
BATCH = 1
SEQ = 256
DEPTH = 1

GRID_W = 64
CTX_LEN = 256
EPS = 1e-6
N_BRANCH = 3
N_MOD = 6

N_HEADS = 16
N_KV_HEADS = 4
HEAD_DIM = 128
GROUP = N_HEADS // N_KV_HEADS
ROPE_PAIRS = HEAD_DIM // 4
ROPE_THETA = 10000.0
Q_BLOCK = 128
Q_WIDTH = N_HEADS * HEAD_DIM
KV_WIDTH = N_KV_HEADS * HEAD_DIM

LRU_WIDTH = D_MODEL
LRU_BLOCKS = 16
LRU_BLOCK = LRU_WIDTH // LRU_BLOCKS
LRU_CONV = 4
LRU_C = 8.0

SC_WIDTH = D_MODEL
SC_CONV = 3

PEER_HEADS = 8
PEER_NKEYS = 128
PEER_EXPERTS = PEER_NKEYS * PEER_NKEYS
PEER_QDIM = 256
PEER_TOPK = 16
PEER_BLOCK = 64

IN_SPLITS = (Q_WIDTH, KV_WIDTH, KV_WIDTH, LRU_WIDTH, LRU_WIDTH, SC_WIDTH, SC_WIDTH, SC_WIDTH, N_BRANCH * D_MODEL)
IN_WIDTH = Q_WIDTH + 2 * KV_WIDTH + 2 * LRU_WIDTH + 3 * SC_WIDTH + N_BRANCH * D_MODEL

kernel_name = 'hybrid_dit_gqa_rglru_shortconv_peer'

def rmsnorm(x, g):
    xf = x.astype(jnp.float32)
    y = xf * lax.rsqrt(jnp.mean(xf * xf, axis=-1, keepdims=True) + EPS)
    return (y * g.astype(jnp.float32)).astype(x.dtype)

def modulate(h, shift, scale):
    return h * (1.0 + scale) + shift

def split_cols(p):
    offsets = np.cumsum(IN_SPLITS)[:-1].tolist()
    return jnp.split(p, offsets, axis=-1)

def dwconv(x, w, b, left):
    k_w = w.shape[0]
    t = x.shape[1]
    xp = jnp.pad(x, ((0, 0), (left, k_w - 1 - left), (0, 0)))
    return b + sum(w[k] * xp[:, k:k + t] for k in range(k_w))

def axial_rope(rows):
    row = jnp.repeat(jnp.arange(rows, dtype=jnp.float32), GRID_W)
    col = jnp.tile(jnp.arange(GRID_W, dtype=jnp.float32), rows)
    inv = ROPE_THETA ** (-jnp.arange(ROPE_PAIRS, dtype=jnp.float32) / ROPE_PAIRS)
    ang = jnp.stack([row[:, None] * inv, col[:, None] * inv], axis=1)
    return jnp.cos(ang), jnp.sin(ang)

def apply_rope(t, cos, sin):
    b_, n_, h_, d_ = t.shape
    t = t.reshape(b_, n_, h_, 2, 2, ROPE_PAIRS)
    t1, t2 = t[..., 0, :], t[..., 1, :]
    cs = cos[:, None].astype(t.dtype)
    sn = sin[:, None].astype(t.dtype)
    out = jnp.stack([t1 * cs - t2 * sn, t2 * cs + t1 * sn], axis=-2)
    return out.reshape(b_, n_, h_, d_)

def attend(q, k, v):
    s = jnp.einsum('bqhgd,bkhd->bhgqk', q, k, preferred_element_type=jnp.float32) * (HEAD_DIM ** -0.5)
    p = jax.nn.softmax(s, axis=-1).astype(v.dtype)
    return jnp.einsum('bhgqk,bkhd->bqhgd', p, v)

def attention_branch(qx, kx, vx, qc, kc, vc, q_gain, k_gain, cos, sin, with_ctx):
    b_, t_, _ = qx.shape
    tc = kc.shape[1]
    ql = apply_rope(rmsnorm(qx.reshape(b_, t_, N_HEADS, HEAD_DIM), q_gain), cos, sin)
    kl = apply_rope(rmsnorm(kx.reshape(b_, t_, N_KV_HEADS, HEAD_DIM), k_gain), cos, sin)
    vl = vx.reshape(b_, t_, N_KV_HEADS, HEAD_DIM)
    kcn = rmsnorm(kc.reshape(b_, tc, N_KV_HEADS, HEAD_DIM), k_gain)
    vcn = vc.reshape(b_, tc, N_KV_HEADS, HEAD_DIM)
    k_all = jnp.concatenate([kcn, kl], axis=1)
    v_all = jnp.concatenate([vcn, vl], axis=1)
    n_blk = t_ // Q_BLOCK
    qb = ql.reshape(b_, n_blk, Q_BLOCK, N_KV_HEADS, GROUP, HEAD_DIM).transpose(1, 0, 2, 3, 4, 5)
    ob = lax.map(lambda q: attend(q, k_all, v_all), qb)
    y_l = ob.transpose(1, 0, 2, 3, 4, 5).reshape(b_, t_, Q_WIDTH)
    y_c = None
    if with_ctx:
        qcn = rmsnorm(qc.reshape(b_, tc, N_HEADS, HEAD_DIM), q_gain)
        y_c = attend(qcn.reshape(b_, tc, N_KV_HEADS, GROUP, HEAD_DIM), kcn, vcn).reshape(b_, tc, Q_WIDTH)
    return y_l, y_c

def _lin_comb(left, right):
    a_l, b_l = left
    a_r, b_r = right
    return a_l * a_r, a_r * b_l + b_r

def rglru_scan(u, wa, ba, wx, bx, lam, h0, reverse):
    b_, t_, c_ = u.shape
    uf = u.astype(jnp.float32)
    ub = uf.reshape(b_, t_, LRU_BLOCKS, LRU_BLOCK)
    r = jax.nn.sigmoid(jnp.einsum('btnc,ncd->btnd', ub, wa.astype(jnp.float32)).reshape(b_, t_, c_) + ba.astype(jnp.float32))
    i = jax.nn.sigmoid(jnp.einsum('btnc,ncd->btnd', ub, wx.astype(jnp.float32)).reshape(b_, t_, c_) + bx.astype(jnp.float32))
    log_a = -LRU_C * r * jax.nn.softplus(-lam.astype(jnp.float32))
    a = jnp.exp(log_a)
    drive = jnp.sqrt(-jnp.expm1(2.0 * log_a)) * (i * uf)
    edge = t_ - 1 if reverse else 0
    drive = drive.at[:, edge].add(a[:, edge] * h0)
    _, h = lax.associative_scan(_lin_comb, (a, drive), axis=1, reverse=reverse)
    return h

def lru_branch(xl, gl, xc, gc, conv_w, conv_b, wa, ba, wx, bx, lam, with_ctx):
    left = LRU_CONV // 2
    ul = dwconv(xl, conv_w, conv_b, left)
    uc = dwconv(xc, conv_w, conv_b, left)
    h_lat = 0.0
    h_ctx = 0.0
    for d, rev in enumerate((False, True)):
        hc_d = rglru_scan(uc, wa[d], ba[d], wx[d], bx[d], lam[d], jnp.zeros((xc.shape[0], LRU_WIDTH), jnp.float32), rev)
        h0 = hc_d[:, 0] if rev else hc_d[:, -1]
        h_lat = h_lat + rglru_scan(ul, wa[d], ba[d], wx[d], bx[d], lam[d], h0, rev)
        if with_ctx:
            h_ctx = h_ctx + hc_d
    y_l = h_lat.astype(xl.dtype) * jax.nn.gelu(gl)
    y_c = h_ctx.astype(xc.dtype) * jax.nn.gelu(gc) if with_ctx else None
    return y_l, y_c

def short_conv(bg, cg, u, w, b):
    return bg * dwconv(cg * u, w, b, SC_CONV // 2)

def merge_branches(att, lru, sc, gate_logits, w_o_attn, w_o_lru, w_o_sc, w_out):
    g_att, g_lru, g_sc = jnp.split(jax.nn.sigmoid(gate_logits), N_BRANCH, axis=-1)
    y = g_att * (att @ w_o_attn) + g_lru * (lru @ w_o_lru) + g_sc * (sc @ w_o_sc)
    return y @ w_out

def peer_ffn(h, w_q, k1, k2, w_u, w_v):
    b_, t_, d_ = h.shape
    n_blk = t_ // PEER_BLOCK
    hb = h.reshape(b_, n_blk, PEER_BLOCK, d_).transpose(1, 0, 2, 3)

    def block(hblk):
        q = (hblk @ w_q).reshape(b_, PEER_BLOCK, PEER_HEADS, 2, PEER_QDIM // 2)
        s1 = jnp.einsum('bthd,hnd->bthn', q[..., 0, :], k1, preferred_element_type=jnp.float32)
        s2 = jnp.einsum('bthd,hnd->bthn', q[..., 1, :], k2, preferred_element_type=jnp.float32)
        v1, i1 = lax.top_k(s1, PEER_TOPK)
        v2, i2 = lax.top_k(s2, PEER_TOPK)
        cand = (v1[..., :, None] + v2[..., None, :]).reshape(b_, PEER_BLOCK, PEER_HEADS, PEER_TOPK * PEER_TOPK)
        cidx = (i1[..., :, None] * PEER_NKEYS + i2[..., None, :]).reshape(b_, PEER_BLOCK, PEER_HEADS, PEER_TOPK * PEER_TOPK)
        score, pos = lax.top_k(cand, PEER_TOPK)
        idx = jnp.take_along_axis(cidx, pos, axis=-1)
        gate = jax.nn.softmax(score, axis=-1)
        u = w_u[idx]
        act = jax.nn.gelu(jnp.einsum('bthkd,btd->bthk', u, hblk))
        return jnp.einsum('bthk,bthkd->btd', (gate * act).astype(h.dtype), w_v[idx])

    out = lax.map(block, hb)
    return out.transpose(1, 0, 2, 3).reshape(b_, t_, d_)

def setup_inputs(seed: int = 0) -> dict:
    key = jax.random.key(seed)
    ks = iter(jax.random.split(key, 40))

    def nrm(shape, scale):
        return scale * jax.random.normal(next(ks), shape, jnp.float32)

    u = jax.random.uniform(next(ks), (DEPTH, 2, LRU_WIDTH), jnp.float32, minval=0.9, maxval=0.999)
    p = u ** (1.0 / LRU_C)
    lam = jnp.log(p) - jnp.log1p(-p)
    return {
        'x': nrm((BATCH, SEQ, D_MODEL), 1.0),
        'c': nrm((BATCH, D_MODEL), 1.0),
        'ctx': nrm((BATCH, CTX_LEN, D_MODEL), 1.0),
        'c_ctx': nrm((D_MODEL,), 1.0),
        'w_mod': nrm((DEPTH, D_MODEL, N_MOD * D_MODEL), 0.5 * D_MODEL ** -0.5),
        'b_mod': nrm((DEPTH, N_MOD * D_MODEL), 0.01),
        'norm_mix': 1.0 + nrm((DEPTH, D_MODEL), 0.02),
        'norm_ffn': 1.0 + nrm((DEPTH, D_MODEL), 0.02),
        'w_in': nrm((DEPTH, D_MODEL, IN_WIDTH), D_MODEL ** -0.5),
        'q_norm': 1.0 + nrm((DEPTH, HEAD_DIM), 0.02),
        'k_norm': 1.0 + nrm((DEPTH, HEAD_DIM), 0.02),
        'lru_conv_w': nrm((DEPTH, LRU_CONV, LRU_WIDTH), LRU_CONV ** -0.5),
        'lru_conv_b': nrm((DEPTH, LRU_WIDTH), 0.01),
        'lru_wa': nrm((DEPTH, 2, LRU_BLOCKS, LRU_BLOCK, LRU_BLOCK), LRU_BLOCK ** -0.5),
        'lru_ba': nrm((DEPTH, 2, LRU_WIDTH), 0.01),
        'lru_wx': nrm((DEPTH, 2, LRU_BLOCKS, LRU_BLOCK, LRU_BLOCK), LRU_BLOCK ** -0.5),
        'lru_bx': nrm((DEPTH, 2, LRU_WIDTH), 0.01),
        'lru_lambda': lam,
        'sc_conv_w': nrm((DEPTH, SC_CONV, SC_WIDTH), SC_CONV ** -0.5),
        'sc_conv_b': nrm((DEPTH, SC_WIDTH), 0.01),
        'w_o_attn': nrm((DEPTH, Q_WIDTH, D_MODEL), Q_WIDTH ** -0.5),
        'w_o_lru': nrm((DEPTH, LRU_WIDTH, D_MODEL), LRU_WIDTH ** -0.5),
        'w_o_sc': nrm((DEPTH, SC_WIDTH, D_MODEL), SC_WIDTH ** -0.5),
        'w_out': nrm((DEPTH, D_MODEL, D_MODEL), D_MODEL ** -0.5),
        'peer_wq': nrm((DEPTH, D_MODEL, PEER_HEADS * PEER_QDIM), D_MODEL ** -0.5),
        'peer_k1': nrm((DEPTH, PEER_HEADS, PEER_NKEYS, PEER_QDIM // 2), (PEER_QDIM // 2) ** -0.5),
        'peer_k2': nrm((DEPTH, PEER_HEADS, PEER_NKEYS, PEER_QDIM // 2), (PEER_QDIM // 2) ** -0.5),
        'peer_u': nrm((DEPTH, PEER_EXPERTS, D_MODEL), D_MODEL ** -0.5),
        'peer_v': nrm((DEPTH, PEER_EXPERTS, D_MODEL), 0.5),
    }

def reference(x, c, ctx, c_ctx, w_mod, b_mod, norm_mix, norm_ffn, w_in, q_norm, k_norm,
              lru_conv_w, lru_conv_b, lru_wa, lru_ba, lru_wx, lru_bx, lru_lambda,
              sc_conv_w, sc_conv_b, w_o_attn, w_o_lru, w_o_sc, w_out,
              peer_wq, peer_k1, peer_k2, peer_u, peer_v):
    rows = x.shape[1] // GRID_W
    cos, sin = axial_rope(rows)
    s_lat = jax.nn.silu(c)
    s_ctx = jax.nn.silu(c_ctx)
    for l in range(DEPTH):
        with_ctx = l < DEPTH - 1
        m_lat = jnp.split((s_lat @ w_mod[l] + b_mod[l])[:, None, :], N_MOD, axis=-1)
        m_ctx = jnp.split(s_ctx @ w_mod[l] + b_mod[l], N_MOD, axis=-1)

        hx = modulate(rmsnorm(x, norm_mix[l]), m_lat[0], m_lat[1])
        hc = modulate(rmsnorm(ctx, norm_mix[l]), m_ctx[0], m_ctx[1])
        qx, kx, vx, lx, lgx, bgx, cgx, ux, gx = split_cols(hx @ w_in[l])
        qc, kc, vc, lc, lgc, bgc, cgc, uc, gc = split_cols(hc @ w_in[l])
        att_x, att_c = attention_branch(qx, kx, vx, qc, kc, vc, q_norm[l], k_norm[l], cos, sin, with_ctx)
        lru_x, lru_c = lru_branch(lx, lgx, lc, lgc, lru_conv_w[l], lru_conv_b[l], lru_wa[l], lru_ba[l],
                                  lru_wx[l], lru_bx[l], lru_lambda[l], with_ctx)
        sc_x = short_conv(bgx, cgx, ux, sc_conv_w[l], sc_conv_b[l])
        x = x + m_lat[2] * merge_branches(att_x, lru_x, sc_x, gx, w_o_attn[l], w_o_lru[l], w_o_sc[l], w_out[l])
        if with_ctx:
            sc_c = short_conv(bgc, cgc, uc, sc_conv_w[l], sc_conv_b[l])
            ctx = ctx + m_ctx[2] * merge_branches(att_c, lru_c, sc_c, gc, w_o_attn[l], w_o_lru[l], w_o_sc[l], w_out[l])

        hx = modulate(rmsnorm(x, norm_ffn[l]), m_lat[3], m_lat[4])
        x = x + m_lat[5] * peer_ffn(hx, peer_wq[l], peer_k1[l], peer_k2[l], peer_u[l], peer_v[l])
        if with_ctx:
            hc = modulate(rmsnorm(ctx, norm_ffn[l]), m_ctx[3], m_ctx[4])
            ctx = ctx + m_ctx[5] * peer_ffn(hc, peer_wq[l], peer_k1[l], peer_k2[l], peer_u[l], peer_v[l])
    return x


_drawn_inputs = setup_inputs


def setup_inputs(seed=0):
    import zlib

    import numpy as np

    out = dict(_drawn_inputs(seed))
    spreads = {}
    factors = {'norm_mix': 4.711,
     'norm_ffn': 39.576,
     'q_norm': 64.0,
     'k_norm': 64.0,
     'lru_conv_b': 21.885,
     'lru_ba': 64.0,
     'lru_bx': 64.0,
     'sc_conv_b': 64.0}
    for name, (base, spread) in spreads.items():
        noise = np.random.default_rng([zlib.crc32(name.encode()), seed]).standard_normal(out[name].shape)
        drawn = base * np.exp(spread * noise) if base else spread * noise
        out[name] = jnp.asarray(drawn.astype(out[name].dtype))
    for name, factor in factors.items():
        out[name] = (out[name] * factor).astype(out[name].dtype)
    return out
```

```python
import numpy as np
import concourse.bass as bass
from concourse import mybir
from contextlib import ExitStack

F32 = mybir.dt.float32
U32 = mybir.dt.uint32
ALU = mybir.AluOpType
ACT = mybir.ActivationFunctionType
AX = mybir.AxisListType

P = 128
D = 2048
KT = D // P
T = 256
CW = 256
HK = KT // 2
NCH = D // CW
HEADS, KVH, HD = 16, 4, 128
GRID_W = 64
ROPE_PAIRS = HD // 4
EPS = 1e-6
LRU_TAPS, SC_TAPS = 4, 3
PH, NKEYS, TOPK = 8, 128, 16
EXPERTS = NKEYS * NKEYS
RING = 4
TINY = 1e-30
LOW = -3.0e38
GELU_A, GELU_S = 0.044715, 2.0 * (2.0 / np.pi) ** 0.5
SCALE = float(HD) ** -0.5

MOD_H = 2 * 2 * NCH
LRU0 = MOD_H
OUT0 = LRU0 + 4 * NCH
KV0 = OUT0 + 4 * NCH
Q0 = KV0 + 8
OUT1 = Q0 + 2 * NCH
SC0 = OUT1 + 4 * NCH
OUT2 = SC0 + 6 * NCH
WO0 = OUT2 + 4 * NCH
WQ0 = WO0 + 2 * NCH
HALVES = WQ0 + 2 * PH

PCOLS, _at = {}, 0
for _name, _n in (("c", 2 * KT), ("b_mod", 2 * KT), ("norm_mix", KT), ("q_norm", 1), ("k_norm", 1),
                  ("lru_w", LRU_TAPS * KT), ("lru_b", KT), ("ba", 2 * KT), ("bx", 2 * KT), ("lam", 2 * KT),
                  ("sc_w", SC_TAPS * KT), ("sc_b", KT)):
    PCOLS[_name] = (_at, _n)
    _at += _n
PW = _at
CC = {"ident": (0, P), "rot": (P, P), "cos": (2 * P, T), "sin": (2 * P + T, T), "iota": (2 * P + 2 * T, TOPK)}
CCW = 2 * P + 2 * T + TOPK


class Steps:

    def __init__(self, sem, names, primed=False):
        self.sem, self.names, self.ahead, self.next = sem, list(names), len(names) if primed else 0, 0
        assert len(set(self.names)) == len(self.names)

    def inc(self, name):
        assert self.names[self.next % len(self.names)] == name, (name, self.names[self.next % len(self.names)])
        self.next += 1
        return self.sem, 1

    def at(self, i, name):
        return self.sem, i * len(self.names) + (self.ahead + self.names.index(name) + 1)


ARENA = 212800


def build(nc, a_stream, a_params, a_consts, a_x, a_ctx, a_gates, a_wmod, a_bmod, a_gffn, a_keys, a_u, a_v, out):
    ctx = ExitStack()
    with ctx:
        m_dram = nc.dram_tensor("m_rows", [4, D], F32, kind="Internal").ap()
        m_flat = m_dram.rearrange("r (c n) -> (r c) n", n=CW)
        x2_dram = nc.dram_tensor("x2_rows", [2, P, D], F32, kind="Internal").ap()

        def sem(name):
            return ctx.enter_context(nc.semaphore(name))

        OFF = -(-nc.sbuf_base // 32) * 32
        ctx.enter_context(nc.sbuf_tensor("arena", [P, ARENA // 4 + 8], F32))

        def sb(name, offset, shape, dt=F32):
            size = int(np.prod(shape[1:])) * 4
            assert offset % 32 == 0 and offset + size <= ARENA, (name, offset, size)
            return nc.alloc_sbuf_tensor_at(name, shape, dt, offset=OFF + offset)

        HB = HK * CW * 4
        W = [sb(f"w{s}", s * HB, [P, HK, CW]) for s in range(RING)]
        R_SPLIT = RING * HB
        R_HX = 65536
        hx = sb("hx", R_HX, [P, KT, T])
        R_HC = 98304
        hc = sb("hc", R_HC, [P, KT, T])
        R_BR = 131072
        br = sb("br", R_BR, [P, KT, T])
        R_Y = 163840
        y = sb("y", R_Y, [P, KT, T])
        R_E = 180224
        R_C = 204800
        par = sb("par", R_C, [P, PW])
        con = sb("con", R_C + 1312, [P, CCW])
        R_D = R_C + 1312 + CCW * 4
        ones = sb("ones", R_D, [P, P])
        sT = sb("sT", R_D + 512, [P, KT, 2])
        mcol = sb("mcol", R_D + 640, [P, 2 * KT, 2])
        cof = sb("cof", R_D + 896, [P, 2, 2 * KT])
        tiny = sb("tiny", R_D + 1152, [P, 2])

        def pc(name, i=0, n=1):
            return par[:, PCOLS[name][0] + i:PCOLS[name][0] + i + n]

        ident = con[:, 0:P]
        rotm = con[:, P:2 * P]
        cosT = con[:, 2 * P:2 * P + T]
        sinT = con[:, 2 * P + T:2 * P + 2 * T]
        iota = con[:, 2 * P + 2 * T:CCW]

        xs = sb("xs", R_BR, [P, 4, D])
        xT = sb("xT", R_Y, [P, KT, 4 * P])
        junk = sb("junk", R_SPLIT, [P, D])
        ssq = sb("ssq", R_SPLIT + 8192, [P, 4])
        rin0 = sb("rin0", R_SPLIT + 8224, [P, 4])
        sig0 = sb("sig0", R_SPLIT + 8256, [P, 2 * KT])
        lm = [sb(f"lm{i}", R_SPLIT + 8448 + 128 * i, [P, 2 * KT]) for i in range(6)]

        o = R_Y
        wg = sb("wg", o, [P, 2, 4, P]); o += 4096
        pad = sb("pad", o, [P, 2, 2, T + LRU_TAPS - 1]); o += 4160
        ub = sb("ub", o, [P, 2, 2 * T]); o += 4096
        tt_ = sb("tt", o, [P, 2, 2 * T]); o += 4096
        aa = sb("aa", o, [P, 2, 2 * T]); o += 4096
        sq = sb("sq", o, [P, 2, 2 * T]); o += 4096
        iu = sb("iu", o, [P, 2, 2 * T]); o += 4096
        hf = sb("hf", o, [P, 2 * T]); o += 2048
        hb = sb("hb", o, [P, 2 * T]); o += 2048
        gp = sb("gp", o, [P, 2 * T]); o += 2048
        gl = sb("gl", o, [P, 2 * T]); o += 2048
        hs = sb("hs", o, [P, T]); o += 1024
        assert o <= R_C

        sg = sb("sg", R_E, [P, 2 * T])
        zt = sb("zt", R_E + 2048, [P, 2 * T])
        mr = [sb(f"mr{i}", R_E + 4096 + i * 8192, [P, HK, CW]) for i in range(2)]
        macc = sb("macc", R_E + 20480, [P, 2, CW])
        brow = sb("brow", R_E + 22528, [P, CW])
        mout = sb("mout", R_E + 23552, [P, CW])

        kT = sb("kT", R_E, [P, KVH, 2 * T])
        vT = sb("vT", R_E + 8192, [P, 4, KVH * HD])
        o = R_HC
        kS = sb("kS", o, [P, 2 * T]); o += 2048
        vS = sb("vS", o, [P, 4, HD]); o += 2048
        nsq = sb("nsq", o, [P, 2 * T]); o += 2048
        nri = sb("nri", o, [P, 2 * T]); o += 2048
        qn = sb("qn", o, [P, 2 * T]); o += 2048
        rt1 = sb("rt1", o, [P, 2 * T]); o += 2048
        rt2 = sb("rt2", o, [P, 2 * T]); o += 2048
        qr = sb("qr", o, [P, 2, 2 * T]); o += 4096
        pr = sb("pr", o, [P, 2, 2 * T]); o += 4096
        pT = sb("pT", o, [P, 2, 4, T]); o += 8192
        st = sb("st", o, [P, 8, 4]); o += 128
        assert o <= R_BR

        cg = sb("cg", R_E, [P, 2 * T])
        cu = sb("cu", R_E + 2048, [P, 2, T + SC_TAPS - 1])
        cv = sb("cv", R_E + 4128, [P, 2, T])

        yf = y
        x2 = sb("x2", R_HX, [P, 2, D])
        xm = sb("xm", R_E, [P, CW])
        hN = sb("hN", R_HX + 16384, [P, 2, D])
        hT = sb("hT", R_HC, [P, KT, T])
        NU, NV = 4, 4
        U = [sb(f"u{i}", R_HC + 16384 + 8192 * i, [P, D]) for i in range(NU)]
        V = [sb(f"v{i}", R_SPLIT + 8192 * i, [P, D]) for i in range(NV)]
        acc = sb("acc", R_HC + 16384 + 8192 * NU, [P, 2, D])
        m2r = sb("m2r", R_HC + 16384, [P, D])
        m3r = sb("m3r", R_HC + 24576, [P, D])
        m4r = sb("m4r", R_BR, [P, D])
        gfr = sb("gfr", R_BR + 8192, [P, D])
        m5r = sb("m5r", R_Y, [P, D])
        x2b = sb("x2b", R_Y + 8192, [P, 2, D])
        o = R_Y + 24576
        keys = sb("keys", o, [P, 2, NKEYS]); o += 1024
        qT = sb("qT", o, [P, 2, T]); o += 2048
        rep = sb("rep", o, [P, 2 * NKEYS]); o += 1024
        cand = sb("cand", o, [P, TOPK, TOPK]); o += 1024
        crep = sb("crep", o, [P, TOPK, TOPK]); o += 1024
        oh = sb("oh", o, [P, TOPK, TOPK]); o += 1024
        dg = sb("dg", o, [P, 4, P]); o += 2048
        tv = sb("tv", o, [P, 2, TOPK]); o += 128
        ti = sb("ti", o, [P, 2, TOPK], U32); o += 128
        tif = sb("tif", o, [P, 2, TOPK]); o += 128
        ts_ = sb("ts_", o, [P, TOPK]); o += 64
        tp = sb("tp", o, [P, TOPK], U32); o += 64
        tph = sb("tph", o, [P, 2, TOPK], U32); o += 128
        tpf = sb("tpf", o, [P, 2, TOPK]); o += 128
        te = sb("te", o, [P, 2, TOPK]); o += 128
        tn = sb("tn", o, [P, 8]); o += 32
        idx = sb("idx", o, [P, 2, TOPK], U32); o += 128
        gate = sb("gate", o, [P, 2, TOPK]); o += 128
        dot = sb("dot", o, [P, 2, TOPK]); o += 128
        gw = sb("gw", o, [P, TOPK]); o += 64
        gs = sb("gs", o, [P, TOPK]); o += 64
        wt = sb("wt", o, [P, 2, TOPK]); o += 128
        assert o <= R_C, o
        fst = sb("fst", R_D + 1184, [P, 8])
        junk2 = sb("junk2", R_Y, [P, D])

        ps = ctx.enter_context(nc.psum_tensor("ps", [P, 8, 2 * T], F32))

        arrived = [sem(f"arrived{s}") for s in range(RING)]
        half_used = sem("half_used")
        apart_count = [sem("apart_dve"), sem("apart_pool")]
        par_in, xs_in = sem("par_in"), sem("xs_in")
        wg_in, x2_in, m_in = sem("wg_in"), sem("x2_in"), sem("m_in")
        mr_in = [sem("mr_in0"), sem("mr_in1")]
        brow_in, m_stored = sem("brow_in"), sem("m_stored")
        rows_in = sem("rows_in")
        keys_in, x2_stored, last_in, stored = sem("keys_in"), sem("x2_stored"), sem("last_in"), sem("stored")
        u_in = [sem(f"u_in{i}") for i in range(NU)]
        v_in = [sem(f"v_in{i}") for i in range(NV)]

        A0 = Steps(sem("act_start"), ["sig", "ez"] + [f"ss{i}" for i in range(4)] + ["rt"])
        V0_ = Steps(sem("dve_start"), ["ones", "tiny", "eps", "st", "neg", "abs", "z2", "rz", "s", "s2", "q0"]
                    + [f"q{i}" for i in range(1, 8)] + ["s1", "mx", "sp", "c4", "c8", "rin"] + [f"xn{i}" for i in range(4)]
                    + [f"xT{k}" for k in range(KT)])
        P0 = Steps(sem("pe_start"), [f"xT{k}" for k in range(KT)])
        VM = Steps(sem("dve_mod"), ["m0", "m1"], primed=True)
        VH = Steps(sem("dve_h"), ["b", "sc"] + [f"{w}{k}" for k in range(KT) for w in ("c", "x")])

        PL = Steps(sem("pe_lru"), [f"g{b}{d}{w}" for b in (0, 1) for d in (0, 1) for w in "ri"], primed=True)
        AL = Steps(sem("act_lru"), ["pad0", "pad1", "gq", "gs"] + [f"{w}{b}" for b in (0, 1)
                   for w in ("r0_", "i0_", "r1_", "i1_", "t0_", "t1_", "e0_", "e1_", "sq")], primed=True)
        VL = Steps(sem("dve_lru"), [f"tap{b}{k}" for b in (0, 1) for k in range(4)] + ["gp", "gx", "gl"]
                   + [f"{w}{b}" for b in (0, 1) for w in ("iu", "rc", "n1", "n2", "a", "dq", "dr", "sf", "sc", "sx", "hs", "ly")],
                   primed=True)
        VZ = Steps(sem("dve_pad"), ["lru", "sc"])
        AO = [Steps(sem(f"act_out{b}"), ["sg"] + (["mo0", "mo1"] if b else []), primed=True) for b in range(3)]
        msteps = [f"m{c}{q}{kk}" for c in (0, 1) for q in (0, 1) for kk in range(HK)]
        msteps.insert(HK * 4, "mb1")
        msteps.insert(HK * 2, "mb0")
        VO = [Steps(sem(f"dve_out{b}"), ["z"] if b == 0 else msteps + ["z", "ya"], primed=True) for b in range(3)]
        PO = [None] + [Steps(sem(f"pe_out{b}"), ["m0", "m1"], primed=True) for b in (1, 2)]
        VK = Steps(sem("dve_kv"), ["v0", "v1", "v2", "v3"] + [f"{w}{h}" for h in range(KVH)
                   for w in ("rc", "kn", "kc", "t1", "t2", "kr")])
        AK = Steps(sem("act_kv"), [f"{w}{h}" for h in range(KVH) for w in ("sq", "rt")])
        PK = Steps(sem("pe_kv"), [f"{w}{h}" for h in range(KVH) for w in ("ss", "rot")])
        units = [(c, hh, qt) for c in (0, 1) for hh in (0, 1) for qt in (0, 1)]

        def ahead_of(first, then, per_head):
            first = (first,) if isinstance(first, str) else first
            names = [f + "%d%d%d" % units[0] for f in first]
            for n, (c, hh, qt) in enumerate(units):
                names += [f + "%d%d%d" % units[n + 1] for f in first if n + 1 < len(units)]
                names += [w + f"{c}{hh}{qt}" for w in then[n]] + ([f"{per_head}{c}{hh}"] if qt and per_head else [])
            return names

        PQ = Steps(sem("pe_q"), ["ss0", "rot0", "ss1", "rot1"]
                   + ahead_of("s", [["t"]] * 8, "o"), primed=True)
        AQ = Steps(sem("act_q"), ["kS", "vS", "sq0", "rt0", "sq1", "rt1"]
                   + ahead_of("ex", [["pt"]] * 8, None), primed=True)
        VQ = Steps(sem("dve_q"), [f"{w}{c}" for c in (0, 1) for w in ("rc", "qn", "t1", "t2", "qr")]
                   + ahead_of(("mx", "nm"), [["rs", "pn"]] * 8, "av"), primed=True)
        AS = Steps(sem("act_sc"), ["cg0", "cg1"], primed=True)
        VS = Steps(sem("dve_sc"), [w for i in (0, 1) for w in [f"cu{i}"] + [f"k{k}{b}_{i}" for k in range(SC_TAPS) for b in (0, 1)] + [f"bg{i}"]], primed=True)
        VW = Steps(sem("dve_wout"), [f"{w}{c}{t}" for c in (0, 1) for t in (0, 1) for w in ("m", "a")], primed=True)
        VF = Steps(sem("dve_ffn"), ["rc0", "g1", "hm0", "ha0", "hm1", "ha1"] + [f"hT{k}" for k in range(KT)] + ["acc0"])
        AF = Steps(sem("act_ffn"), ["ss0", "ss1", "rt"])
        PF = Steps(sem("pe_ffn"), [f"hT{k}" for k in range(KT)])
        PR = Steps(sem("pe_route"), ["s0", "s1"])
        AR = Steps(sem("act_route"), ["q", "ex0", "ex1"])
        top = [f"{w}{s}" for s in (0, 1) for w in ("ma", "ia", "mr", "mb", "ib")]
        VR = Steps(sem("dve_route"), [w + f"_{t}" for t in (0, 1) for w in top + ["cand", "ma2", "ia2", "mr2", "mb2", "ib2",
                   "fi", "hi", "lo", "fp", "o1", "p1", "e1", "o2", "p2", "e2", "nm", "rg", "gt", "idx"]])
        AE = Steps(sem("act_experts"), ["sg0", "sg1"] + [f"dg{t}{k}" for t in (0, 1) for k in range(TOPK)], primed=True)
        VE = Steps(sem("dve_experts"), [w for t in (0, 1) for w in [f"d{t}{k}" for k in range(TOPK)]
                   + [f"{w}{t}" for w in ("g1", "g2", "g3", "g4", "w")]] + ["ac0", "ac1"], primed=True)
        PE_ = Steps(sem("pe_experts"), [f"v{t}{k}" for t in (0, 1) for k in range(TOPK)], primed=True)
        VX = Steps(sem("dve_last"), ["m0", "o0", "m1", "o1"])

        PRIMED_V = [VM, VL] + VO + [VQ, VS, VW, VE]
        PRIMED_A = [AL] + AO + [AQ, AS, AE]
        PRIMED_P = [PL] + PO[1:] + [PQ, PE_]

        block = ctx.enter_context(nc.Block())

        def apart(engine):
            engine.sem_inc(apart_count[engine is nc.gpsimd], 1)

        @block.sync
        def _(sp):
            for s in range(RING):
                sp.dma_start(W[s][:, :, :], a_stream[s].rearrange("p (k n) -> p k n", n=CW)).then_inc(arrived[s], 16)
            with sp.Fori(1, HALVES // RING) as i:
                for s in range(RING):
                    sp.wait_ge(half_used, i * RING + (s - RING + 1))
                    sp.dma_start(W[s][:, :, :], a_stream[bass.ds(i * RING + s, 1), :, :].rearrange("o p (k n) -> (o p) k n", n=CW)).then_inc(arrived[s], 16)
            for t in (0, 1):
                sp.wait_ge(*VX.at(0, f"o{t}"))
                sp.dma_start(out[t], acc[:, t, :]).then_inc(stored, 16)
            sp.wait_ge(stored, 32)

        @block.tensor
        def _(pe):
            for st_ in PRIMED_P:
                pe.sem_inc(st_.sem, st_.ahead)
            mm = nc.tensor.matmul

            def proj(first, turn, h0, outs, moving):
                for q in (0, 1):
                    s = (h0 + q) % RING
                    pe.wait_ge(arrived[s], 16 * (turn + (first + h0 + q) // RING + 1))
                    for kk in range(HK):
                        k = q * HK + kk
                        started = set()
                        for blk in (0, 1):
                            for i, src in enumerate(moving):
                                bank, c0 = outs(blk, i)
                                last = mm(ps[:, bank, c0:c0 + T], W[s][:, kk, blk * P:(blk + 1) * P], src[:, k, :],
                                          start=(k == 0 and bank not in started), stop=(k == KT - 1), skip_group_check=True)
                                started.add(bank)
                    last.then_inc(half_used, 1)

            pe.wait_ge(par_in, 32)
            for k in range(KT):
                if k == 0:
                    pe.wait_ge(*V0_.at(0, "xn3"))
                if k >= 4:
                    pe.wait_ge(*V0_.at(0, f"xT{k - 4}"))
                for t in range(4):
                    last = nc.tensor.transpose(ps[:, 4 + k % 4, t * P:(t + 1) * P], xs[:, t, k * P:(k + 1) * P], ident)
                last.then_inc(*P0.inc(f"xT{k}"))
            pe.wait_ge(*V0_.at(0, "st"))
            with pe.Fori(0, MOD_H // 4) as i:
                for c in (0, 1):
                    pe.wait_ge(*VM.at(i - 1, f"m{c}"))
                    for q in (0, 1):
                        s = 2 * c + q
                        pe.wait_ge(arrived[s], i * 16 + 16)
                        for kk in range(HK):
                            k = q * HK + kk
                            for blk in (0, 1):
                                last = mm(ps[:, c, 2 * blk:2 * blk + 2], W[s][:, kk, blk * P:(blk + 1) * P], sT[:, k, :],
                                          start=(k == 0 and blk == 0), stop=(k == KT - 1), skip_group_check=True)
                        last.then_inc(half_used, 1)

            pe.wait_ge(*VH.at(0, f"x{KT - 1}"))
            with pe.Fori(0, NCH) as j:
                pe.wait_ge(*AL.at(j - 1, "pad1"))
                proj(LRU0, j, 0, lambda blk, i: (blk, i * T), (hc, hx))
                pe.wait_ge(*VL.at(j - 1, "gl"))
                proj(LRU0, j, 2, lambda blk, i: (2, blk * T), (hx,))
                pe.wait_ge(wg_in, j * 16 + 16)
                for b in (0, 1):
                    pe.wait_ge(*VL.at(j, f"tap{b}3"))
                    if b == 0:
                        pe.wait_ge(*AL.at(j - 1, "e1_1"))
                        pe.wait_ge(*VL.at(j - 1, "iu1"))
                    else:
                        pe.wait_ge(*AL.at(j, "e1_0"))
                        pe.wait_ge(*VL.at(j, "iu0"))
                    for d in (0, 1):
                        for w in (0, 1):
                            mm(ps[:, 3 + 2 * w + d, :], wg[:, b, 2 * d + w, :], ub[:, b, :], start=True, stop=True)\
                                .then_inc(*PL.inc(f"g{b}{d}{'ri'[w]}"))

            def out_section(n, h0):
                with pe.Fori(0, NCH) as j:
                    pe.wait_ge(*AO[n].at(j - 1, "sg"))
                    proj(h0, j, 0, lambda blk, i: (0, blk * T), (hx,))
                    if n == 0:
                        pe.wait_ge(*VL.at(NCH - 1, "ly1"))
                        pe.wait_ge(*VO[n].at(j - 1, "z"))
                    elif n == 1:
                        pe.wait_ge(*VQ.at(KVH - 1, "av11"))
                        pe.wait_ge(*VO[n].at(j - 1, "z"))
                    else:
                        pe.wait_ge(*VS.at(NCH // 2 - 1, "bg1"))
                        pe.wait_ge(*VO[n].at(j - 1, "z"))
                    proj(h0, j, 2, lambda blk, i: (1, blk * T), (br,))
                    if n:
                        for c in (0, 1):
                            pe.wait_ge(*VO[n].at(j, f"mb{c}"))
                            pe.wait_ge(*AO[n].at(j - 1, f"mo{c}"))
                            mm(ps[:, 2 + c, 0:CW], ones[:, :], macc[:, c, :], start=True, stop=True).then_inc(*PO[n].inc(f"m{c}"))

            out_section(0, OUT0)

            pe.wait_ge(*VO[0].at(NCH - 1, "z"))
            for c in (0, 1):
                proj(KV0, 0, 2 * c, lambda blk, i: (2 * c + blk, i * T), (hc, hx))
            for c in (0, 1):
                for q in (0, 1):
                    h = 4 + 2 * c + q
                    s = h % RING
                    pe.wait_ge(arrived[s], 16 * ((KV0 + h) // RING + 1))
                    for kk in range(HK):
                        k = q * HK + kk
                        for t in range(4):
                            src = (hc, hx)[t // 2]
                            last = mm(ps[:, 4 + 2 * c + t // 2, (t % 2) * CW:(t % 2 + 1) * CW],
                                      src[:, k, (t % 2) * P:(t % 2 + 1) * P], W[s][:, kk, :],
                                      start=(k == 0 and t % 2 == 0), stop=(k == KT - 1), skip_group_check=True)
                    last.then_inc(half_used, 1)
            for h in range(KVH):
                pe.wait_ge(*AK.at(0, f"sq{h}"))
                pe.wait_ge(*VK.at(0, "v3"))
                mm(ps[:, 4 + 2 * (h % 2), :], ones[:, :], nsq[:, :], start=True, stop=True).then_inc(*PK.inc(f"ss{h}"))
                pe.wait_ge(*VK.at(0, f"kn{h}"))
                mm(ps[:, 5 + 2 * (h % 2), 0:T], rotm, qn[:, T:2 * T], start=True, stop=True).then_inc(*PK.inc(f"rot{h}"))

            pe.wait_ge(*VK.at(0, "kr3"))
            with pe.Fori(0, KVH) as g:
                def ss(c):
                    pe.wait_ge(*AQ.at(g, f"sq{c}"))
                    mm(ps[:, 2, :], ones[:, :], nsq[:, :], start=True, stop=True).then_inc(*PQ.inc(f"ss{c}"))

                def rot(c):
                    pe.wait_ge(*VQ.at(g, f"qn{c}"))
                    mm(ps[:, 3, :], rotm, qn[:, :], start=True, stop=True).then_inc(*PQ.inc(f"rot{c}"))

                pe.wait_ge(*VQ.at(g - 1, "qn0"))
                proj(Q0, g, 0, lambda blk, i: (0, blk * T), (hx,))
                ss(0)
                pe.wait_ge(*VQ.at(g - 1, "qn1"))
                proj(Q0, g, 2, lambda blk, i: (1, blk * T), (hx,))
                rot(0)
                pe.wait_ge(*AQ.at(g, "rt0"))
                ss(1)
                pe.wait_ge(*VQ.at(g, "t20"))
                rot(1)
                pe.wait_ge(*AQ.at(g, "vS"))

                def score(n):
                    c, hh, qt = units[n]
                    pe.wait_ge(*VQ.at(g, f"qr{c}"))
                    if n >= 2:
                        pe.wait_ge(*AQ.at(g, "ex%d%d%d" % units[n - 2]))
                    mm(ps[:, 4 + n % 2, :], qr[:, c, hh * T + qt * P:hh * T + (qt + 1) * P], kS[:, :], start=True, stop=True)\
                        .then_inc(*PQ.inc(f"s{c}{hh}{qt}"))

                score(0)
                for n, (c, hh, qt) in enumerate(units):
                    if n + 1 < len(units):
                        score(n + 1)
                    pe.wait_ge(*VQ.at(g, f"pn{c}{hh}{qt}"))
                    if n:
                        pe.wait_ge(*AQ.at(g, "pt%d%d%d" % units[n - 1]))
                    for kt in range(4):
                        last = nc.tensor.transpose(ps[:, 6, kt * P:(kt + 1) * P], pr[:, n % 2, kt * P:(kt + 1) * P], ident)
                    last.then_inc(*PQ.inc(f"t{c}{hh}{qt}"))
                    if qt:
                        pe.wait_ge(*AQ.at(g, f"pt{c}{hh}1"))
                        if n > 1:
                            pe.wait_ge(*VQ.at(g, "av%d%d" % units[n - 2][:2]))
                        for kt in range(4):
                            last = mm(ps[:, 7, 0:T], vS[:, kt, :], pT[:, hh, kt, :], start=(kt == 0), stop=(kt == 3))
                        last.then_inc(*PQ.inc(f"o{c}{hh}"))

            pe.wait_ge(*VQ.at(KVH - 1, "av11"))
            out_section(1, OUT1)

            pe.wait_ge(*VO[1].at(NCH - 1, "ya"))
            pe.wait_ge(*AO[1].at(NCH - 1, "mo1"))
            with pe.Fori(0, NCH // 2) as i:
                for w in (0, 1):
                    prev = (i, "bg0") if w else (i - 1, "bg1")
                    pe.wait_ge(*VS.at(*prev))
                    for c in range(3):
                        q = 6 * w + 2 * c
                        for hq in (0, 1):
                            s = (q + hq) % RING
                            pe.wait_ge(arrived[s], i * 48 + 16 * ((SC0 + q + hq) // RING + 1))
                            for kk in range(HK):
                                k = hq * HK + kk
                                for blk in (0, 1):
                                    last = mm(ps[:, c, blk * T:(blk + 1) * T], W[s][:, kk, blk * P:(blk + 1) * P], hx[:, k, :],
                                              start=(k == 0 and blk == 0), stop=(k == KT - 1), skip_group_check=True)
                            last.then_inc(half_used, 1)

            pe.wait_ge(*AS.at(NCH // 2 - 1, "cg1"))
            out_section(2, OUT2)

            pe.wait_ge(*VO[2].at(NCH - 1, "ya"))
            with pe.Fori(0, NCH // 2) as i:
                for c in (0, 1):
                    pe.wait_ge(*VW.at(i - 1, f"m{c}1"))
                    for q in (0, 1):
                        s = 2 * c + q
                        pe.wait_ge(arrived[s], i * 16 + 16 * (WO0 // RING + 1))
                        for kk in range(HK):
                            k = q * HK + kk
                            for t in (0, 1):
                                last = mm(ps[:, c, t * CW:(t + 1) * CW], yf[:, k, t * P:(t + 1) * P], W[s][:, kk, :],
                                          start=(k == 0 and t == 0), stop=(k == KT - 1), skip_group_check=True)
                        last.then_inc(half_used, 1)

            for k in range(KT):
                if k == 0:
                    pe.wait_ge(*VF.at(0, "ha1"))
                if k >= 4:
                    pe.wait_ge(*VF.at(0, f"hT{k - 4}"))
                for t in (0, 1):
                    last = nc.tensor.transpose(ps[:, 4 + k % 4, t * P:(t + 1) * P], hN[:, t, k * P:(k + 1) * P], ident)
                last.then_inc(*PF.inc(f"hT{k}"))
            pe.wait_ge(*VF.at(0, f"hT{KT - 1}"))

            def route(turn, slot0):
                for q in (0, 1):
                    s = slot0 + q
                    pe.wait_ge(arrived[s], turn * 16 + 16 * (WQ0 // RING + 1))
                    for kk in range(HK):
                        k = q * HK + kk
                        for blk in (0, 1):
                            last = mm(ps[:, 4, blk * T:(blk + 1) * T], W[s][:, kk, blk * P:(blk + 1) * P], hT[:, k, :],
                                      start=(k == 0 and blk == 0), stop=(k == KT - 1), skip_group_check=True)
                    last.then_inc(half_used, 1)

            def scores(h):
                pe.wait_ge(*AR.at(h, "q"))
                pe.wait_ge(keys_in, h * 16 + 16)
                for t in (0, 1):
                    for s in (0, 1):
                        last = mm(ps[:, 5 + t, s * NKEYS:(s + 1) * NKEYS], qT[:, s, t * P:(t + 1) * P], keys[:, s, :],
                                  start=(s == 0), stop=True, skip_group_check=True)
                    last.then_inc(*PR.inc(f"s{t}"))

            def experts(h):
                for t in (0, 1):
                    for k in range(TOPK):
                        n = t * TOPK + k
                        pe.wait_ge(v_in[n % NV], h * (2 * TOPK // NV * 16) + 16 * (n // NV + 1))
                        pe.wait_ge(*AE.at(h, f"dg{t}{k}"))
                        if k == 0:
                            pe.wait_ge(*(VE.at(h, "ac0") if t else VE.at(h - 1, "ac1")))
                        for b in range(4):
                            last = mm(ps[:, b, :], dg[:, k % 4, :], V[n % NV][:, b * 512:(b + 1) * 512],
                                      start=(k == 0), stop=(k == TOPK - 1))
                        last.then_inc(*PE_.inc(f"v{t}{k}"))

            route(0, 0)
            scores(0)
            with pe.Fori(0, PH // 2 - 1) as i:
                route(i, 2)
                scores(i * 2 + 1)
                experts(i * 2)
                route(i + 1, 0)
                scores(i * 2 + 2)
                experts(i * 2 + 1)
            route(PH // 2 - 1, 2)
            scores(PH - 1)
            experts(PH - 2)
            experts(PH - 1)

        @block.scalar
        def _(act):
            for st_ in PRIMED_A:
                act.sem_inc(st_.sem, st_.ahead)
            fn = nc.scalar.activation
            act.dma_start(par[:, :], a_params).then_inc(par_in, 16)
            act.dma_start(con[:, :], a_consts).then_inc(par_in, 16)
            act.dma_start(xs[:, 0:2, :], a_ctx.rearrange("(t p) d -> p t d", p=P)).then_inc(xs_in, 16)
            act.dma_start(xs[:, 2:4, :], a_x.rearrange("(t p) d -> p t d", p=P)).then_inc(xs_in, 16)
            act.wait_ge(par_in, 32)
            fn(sig0[:, :], pc("c", 0, 2 * KT), ACT.Sigmoid).then_inc(*A0.inc("sig"))
            act.wait_ge(*V0_.at(0, "abs"))
            fn(lm[2][:, :], lm[1][:, :], ACT.Exp, scale=-1.0).then_inc(*A0.inc("ez"))
            act.wait_ge(xs_in, 32)
            for i in range(4):
                if i:
                    act.wait_ge(*A0.at(0, f"ss{i - 1}"))
                fn(junk[:, :], xs[:, i, :], ACT.Square, accum_out=ssq[:, i:i + 1]).then_inc(*A0.inc(f"ss{i}"))
            act.wait_ge(*A0.at(0, "ss3"))
            act.wait_ge(*V0_.at(0, "eps"))
            fn(rin0[:, :], ssq[:, :], ACT.Sqrt, scale=1.0 / D, bias=tiny[:, 1:2]).then_inc(*A0.inc("rt"))

            act.wait_ge(*VH.at(0, f"x{KT - 1}"))
            act.wait_ge(*VZ.at(0, "lru"))
            with act.Fori(0, NCH) as j:
                act.wait_ge(*PL.at(j - 1, "g11i"))
                act.dma_start(wg[:, :, :, :], a_gates[bass.ds(j, 1)].rearrange("o p (b g n) -> (o p) b g n", b=2, g=4)).then_inc(wg_in, 16)
                act.wait_ge(half_used, j * 4 + (LRU0 + 2))
                for b in (0, 1):
                    act.wait_ge(*VL.at(j - 1, f"tap{b}3"))
                    fn(pad[:, b, :, LRU_TAPS // 2:LRU_TAPS // 2 + T], ps[:, b, :].rearrange("p (s t) -> p s t", s=2), ACT.Copy)\
                        .then_inc(*AL.inc(f"pad{b}"))
                act.wait_ge(half_used, j * 4 + (LRU0 + 4))
                act.wait_ge(*VL.at(j - 1, "gl"))
                fn(gp[:, :], ps[:, 2, :], ACT.Square).then_inc(*AL.inc("gq"))
                act.wait_ge(*VL.at(j, "gx"))
                fn(gp[:, :], gp[:, :], ACT.Sigmoid, scale=GELU_S).then_inc(*AL.inc("gs"))
                for b in (0, 1):
                    for d in (0, 1):
                        for w, name in enumerate(("ba", "bx")):
                            act.wait_ge(*PL.at(j, f"g{b}{d}{'ri'[w]}"))
                            fn(ps[:, 3 + 2 * w + d, :], ps[:, 3 + 2 * w + d, :], ACT.Sigmoid,
                               bias=par[:, bass.ds(j * 2 + (PCOLS[name][0] + d * KT + b), 1)]).then_inc(*AL.inc(f"{'ri'[w]}{d}_{b}"))
                    act.wait_ge(*(VL.at(j, "sx0") if b else VL.at(j - 1, "sx1")))
                    act.wait_ge(*AL.at(j, f"i1_{b}"))
                    for d in (0, 1):
                        fn(tt_[:, d, :], ps[:, 3 + d, :], ACT.Tanh, scale=cof[:, 0, bass.ds(j * 2 + (d * KT + b), 1)])\
                            .then_inc(*AL.inc(f"t{d}_{b}"))
                    for d in (0, 1):
                        fn(aa[:, d, :], ps[:, 3 + d, :], ACT.Exp, scale=cof[:, 1, bass.ds(j * 2 + (d * KT + b), 1)])\
                            .then_inc(*AL.inc(f"e{d}_{b}"))
                    act.wait_ge(*AL.at(j, f"t1_{b}"))
                    fn(sq[:, :, :], tt_[:, :, :], ACT.Sqrt, scale=4.0, bias=tiny[:, 0:1]).then_inc(*AL.inc(f"sq{b}"))

            def out_section(n, h0):
                with act.Fori(0, NCH) as j:
                    if n:
                        for c in (0, 1):
                            m = (n - 1) * 2 * NCH + c
                            act.wait_ge(*(VO[n].at(j, "mb0") if c else VO[n].at(j - 1, "mb1")))
                            act.dma_start(brow[0:1, :], a_bmod[bass.ds(j * 2 + m, 1), :]).then_inc(brow_in, 16)
                            for q in (0, 1):
                                act.dma_start(mr[q][:, :, :], a_wmod[bass.ds(j * 4 + (2 * m + q), 1)]
                                              .rearrange("o p (k n) -> (o p) k n", n=CW)).then_inc(mr_in[q], 16)
                    act.wait_ge(half_used, j * 4 + (h0 + 2))
                    act.wait_ge(*VO[n].at(j - 1, "z"))
                    fn(sg[:, :], ps[:, 0, :], ACT.Sigmoid).then_inc(*AO[n].inc("sg"))
                    if n:
                        for c in (0, 1):
                            m = (n - 1) * 2 * NCH + c
                            act.wait_ge(*PO[n].at(j, f"m{c}"))
                            fn(mout[0:1, :], ps[0:1, 2 + c, 0:CW], ACT.Copy).then_inc(*AO[n].inc(f"mo{c}"))
                            act.wait_ge(*AO[n].at(j, f"mo{c}"))
                            act.dma_start(m_flat[bass.ds(j * 2 + m, 1), :], mout[0:1, :]).then_inc(m_stored, 16)
                            act.wait_ge(m_stored, j * 32 + 16 * (m + 1))

            act.wait_ge(*VL.at(NCH - 1, "ly1"))
            out_section(0, OUT0)

            act.wait_ge(half_used, Q0)
            for h in range(KVH):
                if h:
                    act.wait_ge(*PK.at(0, f"ss{h - 1}"))
                fn(nsq[:, :], ps[:, h, :], ACT.Square).then_inc(*AK.inc(f"sq{h}"))
                act.wait_ge(*PK.at(0, f"ss{h}"))
                if h:
                    act.wait_ge(*VK.at(0, f"kn{h - 1}"))
                fn(nri[:, :], ps[:, 4 + 2 * (h % 2), :], ACT.Sqrt, scale=1.0 / HD, bias=tiny[:, 1:2]).then_inc(*AK.inc(f"rt{h}"))

            act.wait_ge(*VK.at(0, "kr3"))
            with act.Fori(0, KVH) as g:
                act.wait_ge(*PQ.at(g - 1, "o11"))
                fn(kS[:, :], kT[:, bass.ds(g, 1), :].rearrange("p o t -> p (o t)"), ACT.Copy).then_inc(*AQ.inc("kS"))
                fn(vS[:, :, :], vT[:, :, bass.ds(g * HD, HD)], ACT.Copy).then_inc(*AQ.inc("vS"))
                for c in (0, 1):
                    act.wait_ge(half_used, g * 4 + (Q0 + 2 * c + 2))
                    act.wait_ge(*(PQ.at(g, "ss0") if c else PQ.at(g - 1, "ss1")))
                    fn(nsq[:, :], ps[:, c, :], ACT.Square).then_inc(*AQ.inc(f"sq{c}"))
                    act.wait_ge(*PQ.at(g, f"ss{c}"))
                    act.wait_ge(*(VQ.at(g, "qn0") if c else VQ.at(g - 1, "qn1")))
                    fn(nri[:, :], ps[:, 2, :], ACT.Sqrt, scale=1.0 / HD, bias=tiny[:, 1:2]).then_inc(*AQ.inc(f"rt{c}"))

                def ex(n):
                    c, hh, qt = units[n]
                    act.wait_ge(*VQ.at(g, f"nm{c}{hh}{qt}"))
                    act.wait_ge(*(PQ.at(g, "t%d%d%d" % units[n - 2]) if n >= 2 else PQ.at(g - 1, "t%d%d%d" % units[6 + n])))
                    fn(pr[:, n % 2, :], ps[:, 4 + n % 2, :], ACT.Exp, scale=SCALE, bias=st[:, n, 1:2], accum_out=st[:, n, 2:3])\
                        .then_inc(*AQ.inc(f"ex{c}{hh}{qt}"))

                ex(0)
                for n, (c, hh, qt) in enumerate(units):
                    if n + 1 < len(units):
                        ex(n + 1)
                    act.wait_ge(*PQ.at(g, f"t{c}{hh}{qt}"))
                    act.wait_ge(*(PQ.at(g, f"o0{hh}") if c else PQ.at(g - 1, f"o1{hh}")))
                    fn(pT[:, hh, :, qt * P:(qt + 1) * P], ps[:, 6, :].rearrange("p (k t) -> p k t", k=4), ACT.Copy)\
                        .then_inc(*AQ.inc(f"pt{c}{hh}{qt}"))

            act.wait_ge(*VQ.at(KVH - 1, "av11"))
            out_section(1, OUT1)

            act.wait_ge(*VZ.at(0, "sc"))
            with act.Fori(0, NCH // 2) as i:
                for w in (0, 1):
                    act.wait_ge(half_used, i * 12 + (SC0 + 6 * w + 2))
                    act.wait_ge(*(VS.at(i, "cu0") if w else VS.at(i - 1, "cu1")))
                    fn(cg[:, :], ps[:, 0, :], ACT.Copy).then_inc(*AS.inc(f"cg{w}"))

            act.wait_ge(*VS.at(NCH // 2 - 1, "bg1"))
            out_section(2, OUT2)

            act.wait_ge(half_used, WO0)
            act.dma_start(x2[:, :, :], a_x.rearrange("(t p) d -> p t d", p=P)).then_inc(x2_in, 16)
            for i, r in enumerate((m2r, m3r, m4r)):
                act.dma_start(r[:, :], m_dram[i:i + 1, :].to_broadcast([P, D])).then_inc(rows_in, 16)
            act.dma_start(gfr[:, :], a_gffn.to_broadcast([P, D])).then_inc(rows_in, 16)
            act.wait_ge(*VW.at(NCH // 2 - 1, "a11"))
            act.wait_ge(half_used, WQ0)
            for t in (0, 1):
                act.dma_start(x2_dram[t], x2[:, t, :]).then_inc(x2_stored, 16)
            for t in (0, 1):
                if t:
                    act.wait_ge(*AF.at(0, "ss0"))
                fn(junk2[:, :], x2[:, t, :], ACT.Square, accum_out=fst[:, t:t + 1]).then_inc(*AF.inc(f"ss{t}"))
            act.wait_ge(*AF.at(0, "ss1"))
            fn(fst[:, 2:4], fst[:, 0:2], ACT.Sqrt, scale=1.0 / D, bias=tiny[:, 1:2]).then_inc(*AF.inc("rt"))
            act.dma_start(keys[:, :, :], a_keys[0].rearrange("p (s n) -> p s n", s=2)).then_inc(keys_in, 16)
            act.dma_start(m5r[:, :], m_dram[3:4, :].to_broadcast([P, D])).then_inc(last_in, 16)
            act.wait_ge(x2_stored, 32)
            act.dma_start(x2b[:, :, :], x2_dram.rearrange("t p d -> p t d")).then_inc(last_in, 16)

            def queries(h, first=False):
                act.wait_ge(half_used, h * 2 + (WQ0 + 2))
                if not first:
                    act.wait_ge(*PR.at(h - 1, "s1"))
                    act.dma_start(keys[:, :, :], a_keys[bass.ds(h, 1)].rearrange("o p (s n) -> (o p) s n", s=2)).then_inc(keys_in, 16)
                fn(qT[:, :, :], ps[:, 4, :].rearrange("p (s t) -> p s t", s=2), ACT.Copy).then_inc(*AR.inc("q"))

            def gates(h, t):
                act.wait_ge(*VR.at(h, f"nm_{t}"))
                fn(gate[:, t, :], ts_[:, :], ACT.Exp, bias=tn[:, 0:1], accum_out=tn[:, 1:2]).then_inc(*AR.inc(f"ex{t}"))

            def gelus(h):
                for t in (0, 1):
                    act.wait_ge(*VE.at(h, f"g3{t}"))
                    fn(gw[:, :], gs[:, :], ACT.Sigmoid, scale=GELU_S).then_inc(*AE.inc(f"sg{t}"))

            def diagonals(h, t):
                act.wait_ge(*VE.at(h, f"w{t}"))
                for k in range(TOPK):
                    n = t * TOPK + k
                    act.wait_ge(*(PE_.at(h, "v%d%d" % divmod(n - 4, TOPK)) if n >= 4 else PE_.at(h - 1, f"v1{TOPK - 4 + k}")))
                    fn(dg[:, k % 4, :], ident, ACT.Copy, scale=wt[:, t, k:k + 1]).then_inc(*AE.inc(f"dg{t}{k}"))

            queries(0, True)
            gates(0, 0)
            gates(0, 1)
            with act.Fori(0, PH - 1) as h:
                queries(h + 1)
                gelus(h)
                diagonals(h, 0)
                gates(h + 1, 0)
                diagonals(h, 1)
                gates(h + 1, 1)
            gelus(PH - 1)
            diagonals(PH - 1, 0)
            diagonals(PH - 1, 1)

        @block.vector
        def _(dve):
            for st_ in PRIMED_V:
                dve.sem_inc(st_.sem, st_.ahead)
            tt, tsc, stt = nc.vector.tensor_tensor, nc.vector.tensor_scalar, nc.vector.scalar_tensor_tensor

            nc.vector.memset(ones[:, :], 1.0).then_inc(*V0_.inc("ones"))
            nc.vector.memset(tiny[:, 0:1], TINY).then_inc(*V0_.inc("tiny"))
            nc.vector.memset(tiny[:, 1:2], EPS).then_inc(*V0_.inc("eps"))
            dve.wait_ge(*A0.at(0, "sig"))
            tt(sT[:, :, :].rearrange("p k v -> p (k v)"), sig0[:, :], pc("c", 0, 2 * KT), ALU.mult).then_inc(*V0_.inc("st"))
            lam = pc("lam", 0, 2 * KT)
            tsc(lm[0][:, :], lam, -1.0, None, ALU.mult).then_inc(*V0_.inc("neg"))
            dve.wait_ge(*V0_.at(0, "neg"))
            tt(lm[1][:, :], lm[0][:, :], lam, ALU.max).then_inc(*V0_.inc("abs"))
            dve.wait_ge(*A0.at(0, "ez"))
            tsc(lm[3][:, :], lm[2][:, :], 2.0, None, ALU.add).then_inc(*V0_.inc("z2"))
            dve.wait_ge(*V0_.at(0, "z2"))
            nc.vector.reciprocal(lm[3][:, :], lm[3][:, :]).then_inc(*V0_.inc("rz"))
            dve.wait_ge(*V0_.at(0, "rz"))
            tt(lm[2][:, :], lm[2][:, :], lm[3][:, :], ALU.mult).then_inc(*V0_.inc("s"))
            dve.wait_ge(*V0_.at(0, "s"))
            tt(lm[3][:, :], lm[2][:, :], lm[2][:, :], ALU.mult).then_inc(*V0_.inc("s2"))
            dve.wait_ge(*V0_.at(0, "s2"))
            tsc(lm[4][:, :], lm[3][:, :], 1.0 / 17, None, ALU.mult).then_inc(*V0_.inc("q0"))
            for i in range(1, 8):
                dve.wait_ge(*V0_.at(0, f"q{i - 1}"))
                stt(lm[4][:, :], lm[4][:, :], 1.0 / (17 - 2 * i), lm[3][:, :], ALU.add, ALU.mult).then_inc(*V0_.inc(f"q{i}"))
            dve.wait_ge(*V0_.at(0, "q7"))
            stt(lm[4][:, :], lm[4][:, :], 1.0, lm[2][:, :], ALU.add, ALU.mult).then_inc(*V0_.inc("s1"))
            tsc(lm[5][:, :], lm[0][:, :], 0.0, None, ALU.max).then_inc(*V0_.inc("mx"))
            dve.wait_ge(*V0_.at(0, "mx"))
            stt(lm[5][:, :], lm[4][:, :], 2.0, lm[5][:, :], ALU.mult, ALU.add).then_inc(*V0_.inc("sp"))
            dve.wait_ge(*V0_.at(0, "sp"))
            tsc(cof[:, 0, :], lm[5][:, :], 4.0, None, ALU.mult).then_inc(*V0_.inc("c4"))
            tsc(cof[:, 1, :], lm[5][:, :], -8.0, None, ALU.mult).then_inc(*V0_.inc("c8"))
            dve.wait_ge(*A0.at(0, "rt"))
            nc.vector.reciprocal(rin0[:, :], rin0[:, :]).then_inc(*V0_.inc("rin"))
            dve.wait_ge(*V0_.at(0, "rin"))
            for i in range(4):
                tsc(xs[:, i, :], xs[:, i, :], rin0[:, i:i + 1], None, ALU.mult).then_inc(*V0_.inc(f"xn{i}"))
            for k in range(KT):
                dve.wait_ge(*P0.at(0, f"xT{k}"))
                nc.vector.tensor_copy(xT[:, k, :], ps[:, 4 + k % 4, :]).then_inc(*V0_.inc(f"xT{k}"))
            with dve.Fori(0, MOD_H // 4) as i:
                for c in (0, 1):
                    dve.wait_ge(half_used, i * 4 + (2 * c + 2))
                    nc.vector.tensor_copy(mcol[:, bass.ds(i * 4 + 2 * c, 2), :], ps[:, c, 0:4].rearrange("p (b v) -> p b v", b=2))\
                        .then_inc(*VM.inc(f"m{c}"))
            dve.wait_ge(*VM.at(MOD_H // 4 - 1, "m1"))
            tt(mcol[:, :, :], mcol[:, :, :], pc("b_mod", 0, 2 * KT).unsqueeze(2).to_broadcast([P, 2 * KT, 2]), ALU.add).then_inc(*VH.inc("b"))
            dve.wait_ge(*VH.at(0, "b"))
            stt(mcol[:, KT:2 * KT, :], mcol[:, KT:2 * KT, :], 1.0, pc("norm_mix", 0, KT).unsqueeze(2).to_broadcast([P, KT, 2]),
                ALU.add, ALU.mult).then_inc(*VH.inc("sc"))
            dve.wait_ge(*VH.at(0, "sc"))
            for k in range(KT):
                tsc(hc[:, k, :], xT[:, k, 0:T], mcol[:, KT + k, 1:2], mcol[:, k, 1:2], ALU.mult, ALU.add).then_inc(*VH.inc(f"c{k}"))
                tsc(hx[:, k, :], xT[:, k, T:2 * T], mcol[:, KT + k, 0:1], mcol[:, k, 0:1], ALU.mult, ALU.add).then_inc(*VH.inc(f"x{k}"))
            dve.wait_ge(*VH.at(0, f"x{KT - 1}"))
            nc.vector.memset(pad[:, :, :, :], 0.0).then_inc(*VZ.inc("lru"))

            with dve.Fori(0, NCH) as j:
                for b in (0, 1):
                    dve.wait_ge(*AL.at(j, f"pad{b}"))
                    dve.wait_ge(*PL.at(j - 1, f"g{b}1i"))
                    uv = ub[:, b, :].rearrange("p (s t) -> p s t", s=2)
                    for k in range(LRU_TAPS):
                        wk = par[:, bass.ds(j * 2 + (PCOLS["lru_w"][0] + k * KT + b), 1)]
                        if k == 0:
                            tsc(uv, pad[:, b, :, 0:T], wk, par[:, bass.ds(j * 2 + (PCOLS["lru_b"][0] + b), 1)],
                                ALU.mult, ALU.add).then_inc(*VL.inc(f"tap{b}0"))
                        else:
                            dve.wait_ge(*VL.at(j, f"tap{b}{k - 1}"))
                            stt(uv, pad[:, b, :, k:k + T], wk, uv, ALU.mult, ALU.add).then_inc(*VL.inc(f"tap{b}{k}"))
                dve.wait_ge(*AL.at(j, "gq"))
                tsc(gp[:, :], gp[:, :], GELU_A, 1.0, ALU.mult, ALU.add).then_inc(*VL.inc("gp"))
                dve.wait_ge(*VL.at(j, "gp"))
                tt(gp[:, :], gp[:, :], ps[:, 2, :], ALU.mult).then_inc(*VL.inc("gx"))
                dve.wait_ge(*AL.at(j, "gs"))
                tt(gl[:, :], gp[:, :], ps[:, 2, :], ALU.mult).then_inc(*VL.inc("gl"))
                for b in (0, 1):
                    dve.wait_ge(*AL.at(j, f"i1_{b}"))
                    tt(iu[:, :, :], ps[:, 5:7, :], ub[:, b:b + 1, :].to_broadcast([P, 2, 2 * T]), ALU.mult).then_inc(*VL.inc(f"iu{b}"))
                    dve.wait_ge(*AL.at(j, f"e1_{b}"))
                    tsc(aa[:, :, :], aa[:, :, :], 1.0, 0.5, ALU.add, ALU.mult).then_inc(*VL.inc(f"rc{b}"))
                    dve.wait_ge(*AL.at(j, f"sq{b}"))
                    dve.wait_ge(*VL.at(j, f"rc{b}"))
                    stt(tt_[:, :, :], tt_[:, :, :], 1.0, aa[:, :, :], ALU.add, ALU.mult).then_inc(*VL.inc(f"n1{b}"))
                    dve.wait_ge(*VL.at(j, f"n1{b}"))
                    stt(aa[:, :, :], tt_[:, :, :], 2.0, aa[:, :, :], ALU.subtract, ALU.mult).then_inc(*VL.inc(f"n2{b}"))
                    dve.wait_ge(*VL.at(j, f"n2{b}"))
                    tsc(tt_[:, :, :], aa[:, :, :], -2.0, -1.0, ALU.mult, ALU.add).then_inc(*VL.inc(f"a{b}"))
                    tt(sq[:, :, :], sq[:, :, :], aa[:, :, :], ALU.mult).then_inc(*VL.inc(f"dq{b}"))
                    dve.wait_ge(*VL.at(j, f"dq{b}"))
                    tt(iu[:, :, :], iu[:, :, :], sq[:, :, :], ALU.mult).then_inc(*VL.inc(f"dr{b}"))
                    dve.wait_ge(*VL.at(j, f"dr{b}"))
                    scan = nc.vector.tensor_tensor_scan
                    scan(hf[:, :], tt_[:, 0, :], iu[:, 0, :], 0.0, ALU.mult, ALU.add).then_inc(*VL.inc(f"sf{b}"))
                    scan(hb[:, T - 1::-1], tt_[:, 1, T - 1::-1], iu[:, 1, T - 1::-1], 0.0, ALU.mult, ALU.add).then_inc(*VL.inc(f"sc{b}"))
                    dve.wait_ge(*VL.at(j, f"sc{b}"))
                    scan(hb[:, 2 * T - 1:T - 1:-1], tt_[:, 1, 2 * T - 1:T - 1:-1], iu[:, 1, 2 * T - 1:T - 1:-1], hb[:, 0:1],
                         ALU.mult, ALU.add).then_inc(*VL.inc(f"sx{b}"))
                    dve.wait_ge(*VL.at(j, f"sx{b}"))
                    tt(hs[:, :], hf[:, T:2 * T], hb[:, T:2 * T], ALU.add).then_inc(*VL.inc(f"hs{b}"))
                    dve.wait_ge(*VL.at(j, f"hs{b}"))
                    stt(br[:, bass.ds(j * 2 + b, 1), :].rearrange("p o t -> p (o t)"), hs[:, :], -1.0, gl[:, b * T:(b + 1) * T],
                        ALU.mult, ALU.mult).then_inc(*VL.inc(f"ly{b}"))

            def out_section(n, h0):
                with dve.Fori(0, NCH) as j:
                    if n:
                        for c in (0, 1):
                            m = (n - 1) * 2 * NCH + c
                            dve.wait_ge(*PO[n].at(j - 1, f"m{c}"))
                            for q in (0, 1):
                                dve.wait_ge(mr_in[q], j * 32 + 16 * (m + 1))
                                for kk in range(HK):
                                    s = sT[:, q * HK + kk, 0:1]
                                    if q == kk == 0:
                                        tsc(macc[:, c, :], mr[q][:, kk, :], s, None, ALU.mult).then_inc(*VO[n].inc(f"m{c}{q}{kk}"))
                                    else:
                                        dve.wait_ge(*VO[n].at(j, f"m{c}%d%d" % divmod(q * HK + kk - 1, HK)))
                                        stt(macc[:, c, :], mr[q][:, kk, :], s, macc[:, c, :], ALU.mult, ALU.add)\
                                            .then_inc(*VO[n].inc(f"m{c}{q}{kk}"))
                            dve.wait_ge(brow_in, j * 32 + 16 * (m + 1))
                            dve.wait_ge(*VO[n].at(j, f"m{c}1{HK - 1}"))
                            tt(macc[0:1, c, :], macc[0:1, c, :], brow[0:1, :], ALU.add).then_inc(*VO[n].inc(f"mb{c}"))
                    dve.wait_ge(half_used, j * 4 + (h0 + 4))
                    dve.wait_ge(*AO[n].at(j, "sg"))
                    yv = y[:, bass.ds(j * 2, 2), :].rearrange("p b t -> p (b t)")
                    if n == 0:
                        tt(yv, ps[:, 1, :], sg[:, :], ALU.mult).then_inc(*VO[n].inc("z"))
                    else:
                        dve.wait_ge(*VO[n].at(j - 1, "ya"))
                        tt(zt[:, :], ps[:, 1, :], sg[:, :], ALU.mult).then_inc(*VO[n].inc("z"))
                        dve.wait_ge(*VO[n].at(j, "z"))
                        tt(yv, yv, zt[:, :], ALU.add).then_inc(*VO[n].inc("ya"))

            dve.wait_ge(*VL.at(NCH - 1, "ly1"))
            out_section(0, OUT0)

            dve.wait_ge(half_used, Q0)
            dve.wait_ge(*VO[0].at(NCH - 1, "z"))
            for i in range(4):
                nc.vector.tensor_copy(vT[:, (i % 2) * 2:(i % 2) * 2 + 2, (i // 2) * CW:(i // 2 + 1) * CW],
                                      ps[:, 4 + i, :].rearrange("p (t n) -> p t n", t=2)).then_inc(*VK.inc(f"v{i}"))
            for h in range(KVH):
                dve.wait_ge(*AK.at(0, f"rt{h}"))
                nc.vector.reciprocal(nri[:, :], nri[:, :]).then_inc(*VK.inc(f"rc{h}"))
                dve.wait_ge(*VK.at(0, f"rc{h}"))
                stt(qn[:, :], ps[:, h, :], pc("k_norm"), nri[:, :], ALU.mult, ALU.mult).then_inc(*VK.inc(f"kn{h}"))
                dve.wait_ge(*VK.at(0, f"kn{h}"))
                nc.vector.tensor_copy(kT[:, h, 0:T], qn[:, 0:T]).then_inc(*VK.inc(f"kc{h}"))
                tt(rt1[:, 0:T], qn[:, T:2 * T], cosT, ALU.mult).then_inc(*VK.inc(f"t1{h}"))
                dve.wait_ge(*PK.at(0, f"rot{h}"))
                tt(rt2[:, 0:T], ps[:, 5 + 2 * (h % 2), 0:T], sinT, ALU.mult).then_inc(*VK.inc(f"t2{h}"))
                dve.wait_ge(*VK.at(0, f"t2{h}"))
                tt(kT[:, h, T:2 * T], rt1[:, 0:T], rt2[:, 0:T], ALU.add).then_inc(*VK.inc(f"kr{h}"))

            dve.wait_ge(*VK.at(0, "kr3"))
            with dve.Fori(0, KVH) as g:
                for c in (0, 1):
                    two = lambda x: x.rearrange("p (h t) -> p h t", h=2)
                    dve.wait_ge(*AQ.at(g, f"rt{c}"))
                    nc.vector.reciprocal(nri[:, :], nri[:, :]).then_inc(*VQ.inc(f"rc{c}"))
                    dve.wait_ge(*VQ.at(g, f"rc{c}"))
                    dve.wait_ge(*(PQ.at(g, "rot0") if c else PQ.at(g - 1, "rot1")))
                    stt(qn[:, :], ps[:, c, :], pc("q_norm"), nri[:, :], ALU.mult, ALU.mult).then_inc(*VQ.inc(f"qn{c}"))
                    dve.wait_ge(*VQ.at(g, f"qn{c}"))
                    tt(two(rt1[:, :]), two(qn[:, :]), cosT.unsqueeze(1).to_broadcast([P, 2, T]), ALU.mult).then_inc(*VQ.inc(f"t1{c}"))
                    dve.wait_ge(*PQ.at(g, f"rot{c}"))
                    tt(two(rt2[:, :]), two(ps[:, 3, :]), sinT.unsqueeze(1).to_broadcast([P, 2, T]), ALU.mult).then_inc(*VQ.inc(f"t2{c}"))
                    dve.wait_ge(*VQ.at(g, f"t2{c}"))
                    dve.wait_ge(*PQ.at(g - 1, f"s{c}11"))
                    tt(qr[:, c, :], rt1[:, :], rt2[:, :], ALU.add).then_inc(*VQ.inc(f"qr{c}"))

                def peak(n):
                    u = "%d%d%d" % units[n]
                    dve.wait_ge(*PQ.at(g, "s" + u))
                    nc.vector.reduce_max(st[:, n, 0:1], ps[:, 4 + n % 2, :], AX.X).then_inc(*VQ.inc("mx" + u))
                    dve.wait_ge(*VQ.at(g, "mx" + u))
                    tsc(st[:, n, 1:2], st[:, n, 0:1], -SCALE, None, ALU.mult).then_inc(*VQ.inc("nm" + u))

                peak(0)
                for n, (c, hh, qt) in enumerate(units):
                    u = f"{c}{hh}{qt}"
                    if n + 1 < len(units):
                        peak(n + 1)
                    dve.wait_ge(*AQ.at(g, "ex" + u))
                    nc.vector.reciprocal(st[:, n, 3:4], st[:, n, 2:3]).then_inc(*VQ.inc("rs" + u))
                    dve.wait_ge(*VQ.at(g, "rs" + u))
                    tsc(pr[:, n % 2, :], pr[:, n % 2, :], st[:, n, 3:4], None, ALU.mult).then_inc(*VQ.inc("pn" + u))
                    if qt:
                        dve.wait_ge(*PQ.at(g, f"o{c}{hh}"))
                        nc.vector.tensor_copy(br[:, bass.ds(g * 4 + (2 * c + hh), 1), :].rearrange("p o t -> p (o t)"), ps[:, 7, 0:T])\
                            .then_inc(*VQ.inc(f"av{c}{hh}"))

            dve.wait_ge(*VQ.at(KVH - 1, "av11"))
            out_section(1, OUT1)

            dve.wait_ge(*VO[1].at(NCH - 1, "ya"))
            nc.vector.memset(cu[:, :, :], 0.0).then_inc(*VZ.inc("sc"))
            dve.wait_ge(*VZ.at(0, "sc"))
            with dve.Fori(0, NCH // 2) as i:
                for w in (0, 1):
                    dve.wait_ge(half_used, i * 12 + (SC0 + 6 * w + 4))
                    dve.wait_ge(*AS.at(i, f"cg{w}"))
                    two = lambda x: x.rearrange("p (b t) -> p b t", b=2)
                    tt(cu[:, :, 1:1 + T], two(cg[:, :]), two(ps[:, 1, :]), ALU.mult).then_inc(*VS.inc(f"cu{w}"))
                    dve.wait_ge(*VS.at(i, f"cu{w}"))
                    for k in range(SC_TAPS):
                        if k:
                            dve.wait_ge(*VS.at(i, f"k{k - 1}1_{w}"))
                        for b in (0, 1):
                            wk = par[:, bass.ds(i * 4 + (PCOLS["sc_w"][0] + k * KT + 2 * w + b), 1)]
                            if k == 0:
                                tsc(cv[:, b, :], cu[:, b, 0:T], wk, par[:, bass.ds(i * 4 + (PCOLS["sc_b"][0] + 2 * w + b), 1)],
                                    ALU.mult, ALU.add).then_inc(*VS.inc(f"k0{b}_{w}"))
                            else:
                                stt(cv[:, b, :], cu[:, b, k:k + T], wk, cv[:, b, :], ALU.mult, ALU.add).then_inc(*VS.inc(f"k{k}{b}_{w}"))
                    dve.wait_ge(half_used, i * 12 + (SC0 + 6 * w + 6))
                    dve.wait_ge(*VS.at(i, f"k21_{w}"))
                    tt(br[:, bass.ds(i * 4 + 2 * w, 2), :].rearrange("p b t -> p (b t)"), cv[:, :, :].rearrange("p b t -> p (b t)"),
                       ps[:, 2, :], ALU.mult).then_inc(*VS.inc(f"bg{w}"))

            dve.wait_ge(*VS.at(NCH // 2 - 1, "bg1"))
            out_section(2, OUT2)

            dve.wait_ge(*VO[2].at(NCH - 1, "ya"))
            dve.wait_ge(x2_in, 16)
            dve.wait_ge(rows_in, 64)
            with dve.Fori(0, NCH // 2) as i:
                for c in (0, 1):
                    dve.wait_ge(half_used, i * 4 + (WO0 + 2 * c + 2))
                    for t in (0, 1):
                        dve.wait_ge(*(VW.at(i, f"a{c}0") if t else (VW.at(i, "a01") if c else VW.at(i - 1, "a11"))))
                        tt(xm[:, :], ps[:, c, t * CW:(t + 1) * CW], m2r[:, bass.ds(i * 512 + c * CW, CW)], ALU.mult).then_inc(*VW.inc(f"m{c}{t}"))
                        dve.wait_ge(*VW.at(i, f"m{c}{t}"))
                        xv = x2[:, t, bass.ds(i * 512 + c * CW, CW)]
                        tt(xv, xv, xm[:, :], ALU.add).then_inc(*VW.inc(f"a{c}{t}"))
            dve.wait_ge(*AF.at(0, "rt"))
            nc.vector.reciprocal(fst[:, 4:6], fst[:, 2:4]).then_inc(*VF.inc("rc0"))
            stt(gfr[:, :], m4r[:, :], 1.0, gfr[:, :], ALU.add, ALU.mult).then_inc(*VF.inc("g1"))
            dve.wait_ge(*VF.at(0, "g1"))
            for t in (0, 1):
                stt(hN[:, t, :], x2[:, t, :], fst[:, 4 + t:5 + t], gfr[:, :], ALU.mult, ALU.mult).then_inc(*VF.inc(f"hm{t}"))
                dve.wait_ge(*VF.at(0, f"hm{t}"))
                tt(hN[:, t, :], hN[:, t, :], m3r[:, :], ALU.add).then_inc(*VF.inc(f"ha{t}"))
            for k in range(KT):
                dve.wait_ge(*PF.at(0, f"hT{k}"))
                nc.vector.tensor_copy(hT[:, k, :], ps[:, 4 + k % 4, 0:T]).then_inc(*VF.inc(f"hT{k}"))
            nc.vector.memset(acc[:, :, :], 0.0).then_inc(*VF.inc("acc0"))
            dve.wait_ge(*VF.at(0, "acc0"))

            def route(h, t, before_idx=lambda: None):
                dve.wait_ge(*PR.at(h, f"s{t}"))
                n = lambda x: x + f"_{t}"

                def top8s(src, copy, vals, inds, names):
                    ma, ia, mr_, mb, ib = (n(x) for x in names)
                    apart(dve)
                    nc.vector.max(vals[:, 0:8], src).then_inc(*VR.inc(ma))
                    dve.wait_ge(*VR.at(h, ma))
                    apart(dve)
                    nc.vector.max_index(inds[:, 0:8], vals[:, 0:8], src).then_inc(*VR.inc(ia))
                    nc.vector.match_replace(copy, vals[:, 0:8], src, LOW).then_inc(*VR.inc(mr_))
                    dve.wait_ge(*VR.at(h, mr_))
                    apart(dve)
                    nc.vector.max(vals[:, 8:16], copy).then_inc(*VR.inc(mb))
                    dve.wait_ge(*VR.at(h, mb))
                    apart(dve)
                    nc.vector.max_index(inds[:, 8:16], vals[:, 8:16], copy).then_inc(*VR.inc(ib))

                for s in (0, 1):
                    top8s(ps[:, 5 + t, s * NKEYS:(s + 1) * NKEYS], rep[:, s * NKEYS:(s + 1) * NKEYS], tv[:, s, :], ti[:, s, :],
                          [f"{w}{s}" for w in ("ma", "ia", "mr", "mb", "ib")])
                dve.wait_ge(*VR.at(h, n("ib1")))
                sq_ = [P, TOPK, TOPK]
                tt(cand[:, :, :], tv[:, 0, :].unsqueeze(2).to_broadcast(sq_), tv[:, 1, :].unsqueeze(1).to_broadcast(sq_), ALU.add)\
                    .then_inc(*VR.inc(n("cand")))
                dve.wait_ge(*VR.at(h, n("cand")))
                flat = lambda x: x[:, :, :].rearrange("p a b -> p (a b)")
                top8s(flat(cand), flat(crep), ts_, tp, ("ma2", "ia2", "mr2", "mb2", "ib2"))
                nc.vector.tensor_copy(tif[:, :, :], ti[:, :, :]).then_inc(*VR.inc(n("fi")))
                dve.wait_ge(*VR.at(h, n("fi")))
                tsc(tph[:, 0, :], tp[:, :], 4, None, ALU.logical_shift_right).then_inc(*VR.inc(n("hi")))
                tsc(tph[:, 1, :], tp[:, :], TOPK - 1, None, ALU.bitwise_and).then_inc(*VR.inc(n("lo")))
                dve.wait_ge(*VR.at(h, n("lo")))
                nc.vector.tensor_copy(tpf[:, :, :], tph[:, :, :]).then_inc(*VR.inc(n("fp")))
                dve.wait_ge(*VR.at(h, n("fp")))
                for s in (0, 1):
                    tt(oh[:, :, :], tpf[:, s, :].unsqueeze(2).to_broadcast(sq_), iota.unsqueeze(1).to_broadcast(sq_), ALU.is_equal)\
                        .then_inc(*VR.inc(n(f"o{s + 1}")))
                    dve.wait_ge(*VR.at(h, n(f"o{s + 1}")))
                    tt(oh[:, :, :], oh[:, :, :], tif[:, s, :].unsqueeze(1).to_broadcast(sq_), ALU.mult).then_inc(*VR.inc(n(f"p{s + 1}")))
                    dve.wait_ge(*VR.at(h, n(f"p{s + 1}")))
                    nc.vector.reduce_sum(te[:, s, :], oh[:, :, :], AX.X).then_inc(*VR.inc(n(f"e{s + 1}")))
                    dve.wait_ge(*VR.at(h, n(f"e{s + 1}")))
                tsc(tn[:, 0:1], ts_[:, 0:1], -1.0, None, ALU.mult).then_inc(*VR.inc(n("nm")))
                dve.wait_ge(*AR.at(h, f"ex{t}"))
                nc.vector.reciprocal(tn[:, 2:3], tn[:, 1:2]).then_inc(*VR.inc(n("rg")))
                dve.wait_ge(*VR.at(h, n("rg")))
                tsc(gate[:, t, :], gate[:, t, :], tn[:, 2:3], None, ALU.mult).then_inc(*VR.inc(n("gt")))
                before_idx()
                stt(idx[:, t, :], te[:, 0, :], float(NKEYS), te[:, 1, :], ALU.mult, ALU.add).then_inc(*VR.inc(n("idx")))

            def gathered(h, t):
                for s in range(NV):
                    last = t * TOPK + TOPK - NV + s
                    dve.wait_ge(v_in[last % NV], h * (2 * TOPK // NV * 16) + 16 * (last // NV + 1))

            def dots(h):
                for t in (0, 1):
                    for k in range(TOPK):
                        n = t * TOPK + k
                        dve.wait_ge(u_in[n % NU], h * (2 * TOPK // NU * 16) + 16 * (n // NU + 1))
                        stt(U[n % NU][:, :], U[n % NU][:, :], 1.0, hN[:, t, :], ALU.mult, ALU.mult, accum_out=dot[:, t, k:k + 1])\
                            .then_inc(*VE.inc(f"d{t}{k}"))
                    dve.wait_ge(*VE.at(h, f"d{t}{TOPK - 1}"))
                    tt(gs[:, :], dot[:, t, :], dot[:, t, :], ALU.mult).then_inc(*VE.inc(f"g1{t}"))
                    dve.wait_ge(*VE.at(h, f"g1{t}"))
                    tsc(gs[:, :], gs[:, :], GELU_A, 1.0, ALU.mult, ALU.add).then_inc(*VE.inc(f"g2{t}"))
                    dve.wait_ge(*VE.at(h, f"g2{t}"))
                    tt(gs[:, :], gs[:, :], dot[:, t, :], ALU.mult).then_inc(*VE.inc(f"g3{t}"))
                    dve.wait_ge(*AE.at(h, f"sg{t}"))
                    tt(gw[:, :], gw[:, :], dot[:, t, :], ALU.mult).then_inc(*VE.inc(f"g4{t}"))
                    dve.wait_ge(*VE.at(h, f"g4{t}"))
                    tt(wt[:, t, :], gw[:, :], gate[:, t, :], ALU.mult).then_inc(*VE.inc(f"w{t}"))

            def add(h, t):
                dve.wait_ge(*PE_.at(h, f"v{t}{TOPK - 1}"))
                tt(acc[:, t, :], acc[:, t, :], ps[:, 0:4, :].rearrange("p b n -> p (b n)"), ALU.add).then_inc(*VE.inc(f"ac{t}"))

            route(0, 0)
            dve.wait_ge(*VR.at(0, "idx_0"))
            route(0, 1)
            dve.wait_ge(*VR.at(0, "idx_1"))
            with dve.Fori(0, PH - 1) as h:
                dots(h)
                route(h + 1, 0, lambda: gathered(h, 0))
                add(h, 0)
                route(h + 1, 1, lambda: gathered(h, 1))
                add(h, 1)
                dve.wait_ge(*VE.at(h, "ac1"))
            dots(PH - 1)
            add(PH - 1, 0)
            add(PH - 1, 1)
            dve.wait_ge(*VE.at(PH - 1, "ac1"))
            dve.wait_ge(last_in, 32)
            for t in (0, 1):
                tt(acc[:, t, :], acc[:, t, :], m5r[:, :], ALU.mult).then_inc(*VX.inc(f"m{t}"))
                dve.wait_ge(*VX.at(0, f"m{t}"))
                tt(acc[:, t, :], acc[:, t, :], x2b[:, t, :], ALU.add).then_inc(*VX.inc(f"o{t}"))

        @block.gpsimd
        def _(pool):
            def gather(table, rows, t, k):
                return nc.gpsimd.indirect_dma_start(out=rows, out_offset=None, in_=table,
                                                    in_offset=bass.IndirectOffsetOnAxis(ap=idx[:, t, k:k + 1], axis=0))

            with pool.Fori(0, PH) as h:
                for t in (0, 1):
                    pool.wait_ge(*VR.at(h, f"idx_{t}"))
                    for k in range(TOPK):
                        n = t * TOPK + k
                        pool.wait_ge(*(VE.at(h, "d%d%d" % divmod(n - NU, TOPK)) if n >= NU else VE.at(h - 1, f"d1{TOPK - NU + k}")))
                        apart(pool)
                        gather(a_u, U[n % NU][:, :], t, k).then_inc(u_in[n % NU], 16)
                for t in (0, 1):
                    for k in range(TOPK):
                        n = t * TOPK + k
                        pool.wait_ge(*(PE_.at(h, "v%d%d" % divmod(n - NV, TOPK)) if n >= NV else PE_.at(h - 1, f"v1{TOPK - NV + k}")))
                        apart(pool)
                        gather(a_v, V[n % NV][:, :], t, k).then_inc(v_in[n % NV], 16)


def kernel(**inputs):
    import concourse.bacc as bacc
    from concourse.bass_utils import run_bass_kernel_spmd as run

    a = {k: np.asarray(v) for k, v in inputs.items()}

    def cols(v):
        v = v.reshape(-1, KT, P)
        return v.transpose(2, 0, 1).reshape(P, -1)

    def halves(w):
        n = w.shape[1] // CW
        return w.reshape(2, HK, P, n, CW).transpose(3, 0, 2, 1, 4).reshape(2 * n, P, HK * CW)

    w_mod, w_in = halves(a["w_mod"][0]), halves(a["w_in"][0])
    q, k, v, lx, lg, bg, cg, u, g0, g1, g2 = (int(x) // CW * 2 for x in np.cumsum(
        [0, D, KVH * HD, KVH * HD] + [D] * 7))
    take = lambda at, n=NCH: w_in[at:at + 2 * n].reshape(n, 2, P, HK * CW)
    chunks = lambda w: halves(w).reshape(NCH, 2, P, HK * CW)
    mix = lambda *parts: np.stack(parts, axis=1).reshape(-1, P, HK * CW)
    stream = np.concatenate([
        w_mod[:MOD_H], mix(take(lx), take(lg)), mix(take(g1), chunks(a["w_o_lru"][0])),
        w_in[k:k + 4], w_in[v:v + 4], w_in[q:q + 2 * NCH], mix(take(g0), chunks(a["w_o_attn"][0])),
        mix(take(cg), take(u), take(bg)), mix(take(g2), chunks(a["w_o_sc"][0])),
        halves(a["w_out"][0]), halves(a["peer_wq"][0])])
    assert len(stream) == HALVES

    cc = np.stack([cols(a["c"])[:, :], cols(a["c_ctx"])], axis=2).reshape(P, 2 * KT)
    params = np.concatenate([
        cc, cols(a["b_mod"][0, :2 * D]), cols(a["norm_mix"]), a["q_norm"].reshape(P, 1), a["k_norm"].reshape(P, 1),
        cols(a["lru_conv_w"][0]), cols(a["lru_conv_b"]), cols(a["lru_ba"][0]), cols(a["lru_bx"][0]), cols(a["lru_lambda"][0]),
        cols(a["sc_conv_w"][0]), cols(a["sc_conv_b"])], axis=1)
    gates = np.stack([a["lru_wa"][0], a["lru_wx"][0]], axis=1)
    gates = gates.reshape(2, 2, NCH, 2, P, P).transpose(2, 4, 3, 0, 1, 5).reshape(NCH, P, -1)
    keys = np.stack([a["peer_k1"][0], a["peer_k2"][0]], axis=1).transpose(0, 3, 1, 2).reshape(PH, P, 2 * NKEYS)

    inv = (10000.0 ** (-np.arange(ROPE_PAIRS, dtype=np.float32) / ROPE_PAIRS)).astype(np.float32)
    pos = np.arange(T)
    row, col = (pos // GRID_W).astype(np.float32), (pos % GRID_W).astype(np.float32)
    angle = np.concatenate([row[:, None] * inv, row[:, None] * inv, col[:, None] * inv, col[:, None] * inv], axis=1).T
    rot = np.zeros((P, P), np.float32)
    for base in (0, 2 * ROPE_PAIRS):
        for i in range(ROPE_PAIRS):
            rot[base + ROPE_PAIRS + i, base + i] = -1.0
            rot[base + i, base + ROPE_PAIRS + i] = 1.0
    consts = np.concatenate([np.eye(P), rot, np.cos(angle.astype(np.float64)), np.sin(angle.astype(np.float64)),
                             np.tile(np.arange(TOPK), (P, 1))], axis=1).astype(np.float32)

    arrays = {
        "stream": stream, "params": params, "consts": consts, "x": a["x"][0], "ctx": a["ctx"][0], "gates": gates,
        "wmod": w_mod[MOD_H:], "bmod": a["b_mod"][0, 2 * D:].reshape(4 * NCH, CW), "gffn": a["norm_ffn"], "keys": keys,
        "peer_u": a["peer_u"][0], "peer_v": a["peer_v"][0],
    }
    nc = bacc.Bacc("TRN2", target_bir_lowering=False, num_devices=1)
    args = []
    for name, x in arrays.items():
        arrays[name] = x = np.ascontiguousarray(x)
        args.append(nc.dram_tensor(f"in_{name}", x.shape, mybir.dt.from_np(x.dtype), kind="ExternalInput").ap())
    args.append(nc.dram_tensor("out", (2, P, D), F32, kind="ExternalOutput").ap())
    build(nc, *args)
    r = run(nc, [{f"in_{k}": v for k, v in arrays.items()}], core_ids=[0])
    return r.results[0]["out"].reshape(1, 2 * P, D)
```

```python
import numpy as np
import concourse.bass as bass
from concourse import mybir
from contextlib import ExitStack

F32 = mybir.dt.float32
F32R = mybir.dt.float32r
U32 = mybir.dt.uint32
ALU = mybir.AluOpType
ACT = mybir.ActivationFunctionType
AX = mybir.AxisListType

P = 128
D = 2048
KT = D // P
T = 256
CW = 256
HK = KT // 2
NCH = D // CW
HEADS, KVH, HD = 16, 4, 128
GRID_W = 64
ROPE_PAIRS = HD // 4
EPS = 1e-6
LRU_TAPS, SC_TAPS = 4, 3
PH, NKEYS, TOPK = 8, 128, 16
EXPERTS = NKEYS * NKEYS
RING = 4
PIECE = HK // 2
SPLITS = 4
AHEAD = 5
TINY = 1e-30
LOW = -3.0e38
GELU_A, GELU_S = 0.044715, 2.0 * (2.0 / np.pi) ** 0.5
SCALE = float(HD) ** -0.5

MOD_H = 2 * 2 * NCH
LRU0 = MOD_H
OUT0 = LRU0 + 4 * NCH
KV0 = OUT0 + 4 * NCH
Q0 = KV0 + 8
OUT1 = Q0 + 2 * NCH
SC0 = OUT1 + 4 * NCH
OUT2 = SC0 + 6 * NCH
WO0 = OUT2 + 4 * NCH
WQ0 = WO0 + 2 * NCH
HALVES = WQ0 + 2 * PH

PCOLS, _at = {}, 0
for _name, _n in (("c", 2 * KT), ("b_mod", 2 * KT), ("norm_mix", KT), ("q_norm", 1), ("k_norm", 1),
                  ("lru_w", LRU_TAPS * KT), ("lru_b", KT), ("ba", 2 * KT), ("bx", 2 * KT), ("lam", 2 * KT),
                  ("sc_w", SC_TAPS * KT), ("sc_b", KT)):
    PCOLS[_name] = (_at, _n)
    _at += _n
PW = _at
CC = {"ident": (0, P), "rot": (P, P), "cos": (2 * P, T), "sin": (2 * P + T, T), "iota": (2 * P + 2 * T, TOPK)}
CCW = 2 * P + 2 * T + TOPK


class Steps:

    def __init__(self, sem, names, primed=False):
        self.sem, self.names, self.ahead, self.next = sem, list(names), len(names) if primed else 0, 0
        assert len(set(self.names)) == len(self.names)

    def inc(self, name):
        assert self.names[self.next % len(self.names)] == name, (name, self.names[self.next % len(self.names)])
        self.next += 1
        return self.sem, 1

    def at(self, i, name):
        return self.sem, i * len(self.names) + (self.ahead + self.names.index(name) + 1)


ARENA = 212800


def build(nc, a_stream, a_params, a_consts, a_x, a_ctx, a_gates, a_wmod, a_bmod, a_gffn, a_keys, a_u, a_v, out):
    ctx = ExitStack()
    with ctx:
        m_dram = nc.dram_tensor("m_rows", [4, D], F32, kind="Internal").ap()
        m_flat = m_dram.rearrange("r (c n) -> (r c) n", n=CW)
        x2_dram = nc.dram_tensor("x2_rows", [2, P, D], F32, kind="Internal").ap()

        def sem(name):
            return ctx.enter_context(nc.semaphore(name))

        OFF = -(-nc.sbuf_base // 32) * 32
        ctx.enter_context(nc.sbuf_tensor("arena", [P, ARENA // 4 + 8], F32))

        def sb(name, offset, shape, dt=F32):
            size = int(np.prod(shape[1:])) * 4
            assert offset % 32 == 0 and offset + size <= ARENA, (name, offset, size)
            return nc.alloc_sbuf_tensor_at(name, shape, dt, offset=OFF + offset)

        HB = HK * CW * 4
        W = [sb(f"w{s}", s * HB, [P, HK, CW]) for s in range(RING)]
        R_SPLIT = RING * HB
        PB = PIECE * CW * 4
        wh = [sb(f"wh{i}", R_SPLIT + i * PB, [P, PIECE, CW], F32R) for i in range(SPLITS)]
        wl = [sb(f"wl{i}", R_SPLIT + (SPLITS + i) * PB, [P, PIECE, CW], F32R) for i in range(SPLITS)]
        R_HX = 65536
        pair = lambda name, at: [sb(name + w, at + i * KT * T * 4, [P, KT, T], F32R) for i, w in enumerate(("_hi", "_lo"))]
        hx = pair("hx", R_HX)
        R_HC = 98304
        hc = pair("hc", R_HC)
        R_BR = 131072
        br = pair("br", R_BR)
        R_Y = 163840
        y = sb("y", R_Y, [P, KT, T])
        R_E = 180224
        R_C = 204800
        par = sb("par", R_C, [P, PW])
        con = sb("con", R_C + 1312, [P, CCW])
        R_D = R_C + 1312 + CCW * 4
        ones = sb("ones", R_D, [P, P])
        sT = sb("sT", R_D + 512, [P, KT, 2])
        mcol = sb("mcol", R_D + 640, [P, 2 * KT, 2])
        cof = sb("cof", R_D + 896, [P, 2, 2 * KT])
        tiny = sb("tiny", R_D + 1152, [P, 2])

        def pc(name, i=0, n=1):
            return par[:, PCOLS[name][0] + i:PCOLS[name][0] + i + n]

        ident = con[:, 0:P]
        rotm = con[:, P:2 * P]
        cosT = con[:, 2 * P:2 * P + T]
        sinT = con[:, 2 * P + T:2 * P + 2 * T]
        iota = con[:, 2 * P + 2 * T:CCW]

        xs = sb("xs", R_BR, [P, 4, D])
        xT = sb("xT", R_Y, [P, KT, 4 * P])
        junk = sb("junk", R_SPLIT, [P, D])
        ssq = sb("ssq", R_SPLIT + 8192, [P, 4])
        rin0 = sb("rin0", R_SPLIT + 8224, [P, 4])
        sig0 = sb("sig0", R_SPLIT + 8256, [P, 2 * KT])
        mrow = sb("mrow", R_SPLIT + 16384, [P, 2 * D])
        lm = [sb(f"lm{i}", R_SPLIT + 8448 + 128 * i, [P, 2 * KT]) for i in range(6)]

        o = R_Y
        wg = sb("wg", o, [P, 2, 4, P]); o += 4096
        pad = sb("pad", o, [P, 2, 2, T + LRU_TAPS - 1]); o += 4160
        ub = sb("ub", o, [P, 2, 2 * T]); o += 4096
        tt_ = sb("tt", o, [P, 2, 2 * T]); o += 4096
        aa = sb("aa", o, [P, 2, 2 * T]); o += 4096
        sq = sb("sq", o, [P, 2, 2 * T]); o += 4096
        iu = sb("iu", o, [P, 2, 2 * T]); o += 4096
        hf = sb("hf", o, [P, 2 * T]); o += 2048
        hb = sb("hb", o, [P, 2 * T]); o += 2048
        gp = sb("gp", o, [P, 2 * T]); o += 2048
        gl = sb("gl", o, [P, 2 * T]); o += 2048
        hs = sb("hs", o, [P, T]); o += 1024
        sg0 = sb("sg0", R_C - 2048, [P, 2 * T])
        assert o <= R_C - 2048

        sg = sb("sg", R_E, [P, 2 * T])
        zt = sb("zt", R_E + 2048, [P, 2 * T])
        mr = [sb(f"mr{i}", R_E + 4096 + i * 8192, [P, HK, CW]) for i in range(2)]
        macc = sb("macc", R_E + 20480, [P, CW])
        brow = sb("brow", R_E + 21504, [P, CW])
        mout = sb("mout", R_D + 1216, [P, CW])

        kT = sb("kT", R_E, [P, KVH, 2 * T])
        vT = sb("vT", R_E + 8192, [P, 4, KVH * HD])
        o = R_HC
        kS = sb("kS", o, [P, 2 * T]); o += 2048
        vS = sb("vS", o, [P, 4, HD]); o += 2048
        nsq = sb("nsq", o, [P, 2 * T]); o += 2048
        nri = sb("nri", o, [P, 2 * T]); o += 2048
        qn = sb("qn", o, [P, 2 * T]); o += 2048
        rt1 = sb("rt1", o, [P, 2 * T]); o += 2048
        rt2 = sb("rt2", o, [P, 2 * T]); o += 2048
        qr = sb("qr", o, [P, 2, 2 * T]); o += 4096
        pr = sb("pr", o, [P, 3, 2 * T]); o += 6144
        pT = sb("pT", o, [P, 2, 4, T]); o += 8192
        st = sb("st", R_D + 3264, [P, 8, 4])
        assert o <= R_BR

        cg = sb("cg", R_HC, [P, 2 * T])
        cu = sb("cu", R_HC + 2048, [P, 2, T + SC_TAPS - 1])
        cv = sb("cv", R_HC + 4128, [P, 2, T])
        cb = sb("cb", R_HC + 6176, [P, 2 * T])

        yf = pair("y", R_HC)
        x2 = sb("x2", R_HX, [P, 2, D])
        xm = sb("xm", R_E, [P, CW])
        hN = sb("hN", R_HX + 16384, [P, 2, D])
        hT = sb("hT", R_HC, [P, KT, T])
        NU, NV = 4, 8
        U = [sb(f"u{i}", R_HC + 16384 + 8192 * i, [P, D]) for i in range(NU)]
        V = [sb(f"v{i}", at, [P, D]) for i, at in enumerate(
            [R_SPLIT + 8192 * i for i in range(4)] + [R_HX, R_HX + 8192, R_Y + 8192, R_Y + 16384])]
        acc = sb("acc", R_HC + 16384 + 8192 * NU, [P, 2, D])
        m2r = sb("m2r", R_Y, [P, D])
        m3r = sb("m3r", R_Y + 8192, [P, D])
        m4r = sb("m4r", R_BR, [P, D])
        gfr = sb("gfr", R_BR + 8192, [P, D])
        m5r = sb("m5r", R_Y, [P, D])
        x2b = sb("x2b", R_HC + 16384, [P, 2, D])
        o = R_Y + 24576
        keys = sb("keys", o, [P, 2, NKEYS]); o += 1024
        qT = sb("qT", o, [P, 2, T]); o += 2048
        rep = sb("rep", o, [P, 2 * NKEYS]); o += 1024
        cand = sb("cand", o, [P, TOPK, TOPK]); o += 1024
        crep = sb("crep", o, [P, TOPK, TOPK]); o += 1024
        oh = sb("oh", o, [P, TOPK, TOPK]); o += 1024
        dg = sb("dg", o, [P, 4, P]); o += 2048
        tv = sb("tv", o, [P, 2, TOPK]); o += 128
        ti = sb("ti", o, [P, 2, TOPK], U32); o += 128
        tif = sb("tif", o, [P, 2, TOPK]); o += 128
        ts_ = sb("ts_", o, [P, TOPK]); o += 64
        tp = sb("tp", o, [P, TOPK], U32); o += 64
        tph = sb("tph", o, [P, 2, TOPK], U32); o += 128
        tpf = sb("tpf", o, [P, 2, TOPK]); o += 128
        te = sb("te", o, [P, 2, TOPK]); o += 128
        tn = sb("tn", o, [P, 8]); o += 32
        idx = sb("idx", o, [P, 2, 2, TOPK], U32); o += 256
        gate = sb("gate", o, [P, 2, TOPK]); o += 128
        dot = sb("dot", o, [P, 2, TOPK]); o += 128
        gw = sb("gw", o, [P, TOPK]); o += 64
        gs = sb("gs", o, [P, TOPK]); o += 64
        wt = sb("wt", o, [P, 2, TOPK]); o += 128
        assert o <= R_C, o
        fst = sb("fst", R_D + 1184, [P, 8])
        junk2 = sb("junk2", R_BR + 16384, [P, D])

        ps = ctx.enter_context(nc.psum_tensor("ps", [P, 8, 2 * T], F32))

        arrived = [sem(f"arrived{s}") for s in range(RING)]
        piece_used = sem("piece_used")
        hi_done, lo_done = sem("hi_done"), sem("lo_done")
        apart_count = [sem("apart_dve"), sem("apart_pool")]
        par_in, xs_in = sem("par_in"), sem("xs_in")
        wg_in, x2_in, m_in = sem("wg_in"), sem("x2_in"), sem("m_in")
        mr_in = [sem("mr_in0"), sem("mr_in1")]
        brow_in, m_stored = sem("brow_in"), sem("m_stored")
        rows_in = sem("rows_in")
        keys_in, x2_stored, last_in, stored = sem("keys_in"), sem("x2_stored"), sem("last_in"), sem("stored")
        u_in = [sem(f"u_in{i}") for i in range(NU)]
        v_in = [sem(f"v_in{i}") for i in range(NV)]

        A0 = Steps(sem("act_start"), ["sig", "ez"] + [f"ss{i}" for i in range(4)] + ["rt"])
        V0_ = Steps(sem("dve_start"), ["ones", "tiny", "eps", "st", "neg", "abs", "z2", "rz", "s", "s2", "q0"]
                    + [f"q{i}" for i in range(1, 8)] + ["s1", "mx", "sp", "c4", "c8", "rin"] + [f"xn{i}" for i in range(4)]
                    + [f"xT{k}" for k in range(KT)])
        PM = Steps(sem("pe_mod"), ["rows"])
        AH = Steps(sem("act_h"), [f"{w}{k}" for k in range(KT) for w in ("c", "x")])
        P0 = Steps(sem("pe_start"), [f"xT{k}" for k in range(KT)])
        VM = Steps(sem("dve_mod"), ["m0", "m1"], primed=True)
        LAG = 2
        VH = Steps(sem("dve_h"), ["col", "b", "sc"] + [w for k in range(KT + LAG) for w in
                   [f"{w}{k}" for w in "cx" if k < KT] + [f"lo_{w}{k - LAG}" for w in "cx" if k >= LAG]])

        PL = Steps(sem("pe_lru"), [f"g{b}{d}{w}" for b in (0, 1) for d in (0, 1) for w in "ri"], primed=True)
        AL = Steps(sem("act_lru"), ["pad0", "pad1"] + [w for b in (0, 1) for w in ([] if b == 0 else ["gq", "gs"])
                   + [f"{w}{b}" for w in ("r0_", "i0_", "r1_", "i1_", "t0_", "t1_", "e0_", "e1_", "sq")]], primed=True)
        VL = Steps(sem("dve_lru"), [f"tap{b}{k}" for b in (0, 1) for k in range(4)]
                   + [w for b in (0, 1) for w in [f"{w}{b}" for w in ("iu", "rc", "n1", "n2", "a", "dq", "dr", "sf", "sc", "sx", "hs")]
                      + ([] if b else ["gp", "gx", "gl"]) + [f"{w}{b}" for w in ("ly", "bh", "bl")]],
                   primed=True)
        VZ = Steps(sem("dve_pad"), ["lru", "sc"])
        AO = [Steps(sem(f"act_out{b}"), ["sg"], primed=True) for b in range(3)]
        VO = [Steps(sem(f"dve_out{b}"), ["z"] + ["ya"] * (b > 0) + ["yh", "yl"] * (b == 2), primed=True) for b in range(3)]
        VC = Steps(sem("dve_chunk"), [f"k{k}" for k in range(KT)] + ["b"], primed=True)
        PC = Steps(sem("pe_chunk"), ["m"], primed=True)
        AC = Steps(sem("act_chunk"), ["mo"], primed=True)
        VK = Steps(sem("dve_kv"), ["v0", "v1", "v2", "v3"] + [f"{w}{h}" for h in range(KVH)
                   for w in ("rc", "kn", "kc", "t1", "t2", "kr")])
        AK = Steps(sem("act_kv"), [f"{w}{h}" for h in range(KVH) for w in ("sq", "rt")])
        PK = Steps(sem("pe_kv"), [f"{w}{h}" for h in range(KVH) for w in ("ss", "rot")])
        SB = (4, 5, 2)
        units = [(c, hh, qt) for c in (0, 1) for hh in (0, 1) for qt in (0, 1)]

        def of_half(name, units_, c):
            return [f"{name}{c}{hh}{qt}" for hh, qt in (divmod(n, 2) for n in units_)]

        PN = Steps(sem("pe_qnorm"), ["ss", "rot"], primed=True)
        AN = Steps(sem("act_qnorm"), ["sq", "rt"], primed=True)
        VN = Steps(sem("dve_qnorm"), ["rc", "qn", "t1", "t2", "qr"], primed=True)
        PQ = Steps(sem("pe_q"), [w for c in (0, 1) for w in
                   of_half("s", (0, 1, 2), c) + of_half("t", (0,), c) + of_half("s", (3,), c) + of_half("t", (1,), c) + [f"o{c}0"]
                   + of_half("t", (2, 3), c) + [f"o{c}1"]], primed=True)
        AQ = Steps(sem("act_q"), [w for c in (0, 1) for w in
                   of_half("ex", (0, 1, 2), c) + of_half("pt", (0,), c) + of_half("ex", (3,), c) + of_half("pt", (1, 2, 3), c)], primed=True)
        two_steps = lambda a, b, n, c: of_half(a, (n,), c) + of_half(b, (n,), c)
        VQ = Steps(sem("dve_q"), [w for c in (0, 1) for w in
                   two_steps("mx", "nm", 0, c) + two_steps("mx", "nm", 1, c) + two_steps("rs", "pn", 0, c)
                   + two_steps("mx", "nm", 2, c) + two_steps("rs", "pn", 1, c) + two_steps("mx", "nm", 3, c)
                   + two_steps("rs", "pn", 2, c) + [f"av{c}0", f"al{c}0"] + two_steps("rs", "pn", 3, c) + [f"av{c}1", f"al{c}1"]],
                   primed=True)
        staged = sem("staged")
        AS = Steps(sem("act_sc"), ["cg0", "cg1"], primed=True)
        VS = Steps(sem("dve_sc"), [w for i in (0, 1) for w in [f"cu{i}"] + [f"k{k}{b}_{i}" for k in range(SC_TAPS) for b in (0, 1)] + [f"{w}{i}" for w in ("bg", "bh", "bl")]], primed=True)
        VW = Steps(sem("dve_wout"), [f"{w}{c}{t}" for c in (0, 1) for t in (0, 1) for w in ("m", "a")], primed=True)
        VF = Steps(sem("dve_ffn"), ["g1", "rc0"] + [f"{w}{t}{half}" for half in (0, 1) for t in (0, 1) for w in ("hm", "ha")] + ["acc0"])
        AF = Steps(sem("act_ffn"), ["ss0", "ss1", "rt"] + [f"hT{k}" for k in range(KT)])
        PF = Steps(sem("pe_ffn"), [f"hT{k}" for k in range(KT)])
        PR = Steps(sem("pe_route"), ["s0", "s1"])
        AR = Steps(sem("act_queries"), ["q"])
        AX_ = Steps(sem("act_gates"), ["ex0", "ex1"])
        top = [f"{w}{s}" for s in (0, 1) for w in ("ma", "ia", "mr", "mb", "ib")]
        VR = Steps(sem("dve_route"), [w + f"_{t}" for t in (0, 1) for w in top + ["cand", "ma2", "ia2", "mr2", "mb2", "ib2",
                   "fi", "hi", "lo", "fp", "o1", "p1", "e1", "o2", "p2", "e2", "nm", "rg", "gt", "idx"]])
        AG = Steps(sem("act_gelu"), ["sg0", "sg1"])
        AE = Steps(sem("act_experts"), [f"dg{t}{k}" for t in (0, 1) for k in range(TOPK)], primed=True)
        VE = Steps(sem("dve_experts"), [w for t in (0, 1) for w in [f"d{t}{k}" for k in range(TOPK)]
                   + [f"{w}{t}" for w in ("g1", "g2", "g3", "g4", "w")]], primed=True)
        VA = Steps(sem("dve_adds"), ["ac0", "ac1"], primed=True)
        PE_ = Steps(sem("pe_experts"), [f"v{t}{k}" for t in (0, 1) for k in range(TOPK)], primed=True)
        VX = Steps(sem("dve_last"), ["m0", "o0", "m1", "o1"])

        PRIMED_V = [VM, VL, VC] + VO + [VN, VQ, VS, VW, VE, VA]
        PRIMED_A = [AL] + AO + [AC, AN, AQ, AS, AE]
        PRIMED_P = [PL, PC, PN, PQ, PE_]

        block = ctx.enter_context(nc.Block())

        def apart(engine):
            engine.sem_inc(apart_count[engine is nc.gpsimd], 1)

        @block.sync
        def _(sp):
            for s in range(RING):
                sp.dma_start(W[s][:, :, :], a_stream[s].rearrange("p (k n) -> p k n", n=CW)).then_inc(arrived[s], 16)

            def load(i, s):
                sp.dma_start(W[s][:, :, :], a_stream[bass.ds(i * RING + s, 1), :, :].rearrange("o p (k n) -> (o p) k n", n=CW))\
                    .then_inc(arrived[s], 16)

            def by_pe(i0, i1):
                with sp.Fori(i0, i1) as i:
                    for s in range(RING):
                        sp.wait_ge(piece_used, i * (2 * RING) + 2 * (s - RING + 1))
                        load(i, s)

            by_pe(1, LRU0 // RING + 1)
            with sp.Fori(LRU0 // RING + 1, WQ0 // RING + 1) as i:
                for s in range(RING):
                    sp.wait_ge(lo_done, i * (2 * RING) + 2 * (s - RING + 1 - LRU0))
                    load(i, s)
            by_pe(WQ0 // RING + 1, HALVES // RING)
            for t in (0, 1):
                sp.wait_ge(*VX.at(0, f"o{t}"))
                sp.dma_start(out[t], acc[:, t, :]).then_inc(stored, 16)
            sp.wait_ge(stored, 32)

        @block.tensor
        def _(pe):
            for st_ in PRIMED_P:
                pe.sem_inc(st_.sem, st_.ahead)
            mm = nc.tensor.matmul

            def pieces(first, turn, per, p0, n):
                for p in range(p0, p0 + n):
                    pe.wait_ge(lo_done, turn * per + 2 * (first - LRU0) + p + 1)
                    yield (p - p0) * PIECE, wh[p % SPLITS], wl[p % SPLITS]

            def proj(first, turn, p0, outs, moving, per=8, part=range(4)):
                for p in part:
                    (k0, hi, lo), = pieces(first, turn, per, p0 + p, 1)
                    for kk in range(PIECE):
                        k = p * PIECE + kk
                        started = set()
                        for blk in (0, 1):
                            cols = slice(blk * P, (blk + 1) * P)
                            for w, parts in ((hi, (0, 1)), (lo, (0,))):
                                for i, src in enumerate(moving):
                                    bank, c0 = outs(blk, i)
                                    for part_ in parts:
                                        last = mm(ps[:, bank, c0:c0 + T], w[:, kk, cols], src[part_][:, k, :],
                                                  start=(k == 0 and bank not in started), stop=(k == KT - 1), skip_group_check=True)
                                        started.add(bank)
                    last.then_inc(piece_used, 1)

            def tokens(first, turn, per, p0, outs, still):
                for p in range(4):
                    (k0, hi, lo), = pieces(first, turn, per, p0 + p, 1)
                    for kk in range(PIECE):
                        k = p * PIECE + kk
                        for t, (src, tile) in enumerate(still):
                            out_, first_in_bank = outs(t)
                            cols = slice(tile * P, (tile + 1) * P)
                            mm(out_, src[0][:, k, cols], hi[:, kk, :], start=(k == 0 and first_in_bank), stop=False, skip_group_check=True)
                            mm(out_, src[0][:, k, cols], lo[:, kk, :], start=False, stop=False, skip_group_check=True)
                            last = mm(out_, src[1][:, k, cols], hi[:, kk, :], start=False, stop=(k == KT - 1), skip_group_check=True)
                    last.then_inc(piece_used, 1)

            def mod_turns(i0, i1):
                with pe.Fori(i0, i1) as i:
                    for c in (0, 1):
                        pe.wait_ge(*VM.at(i - 1, f"m{c}"))
                        for q in (0, 1):
                            s = 2 * c + q
                            pe.wait_ge(arrived[s], i * 16 + 16)
                            for kk in range(HK):
                                k = q * HK + kk
                                last = mm(ps[0:2, c, 0:CW], sT[:, k, :], W[s][:, kk, :], start=(k == 0), stop=(k == KT - 1))
                            last.then_inc(piece_used, 2)

            pe.wait_ge(*V0_.at(0, "st"))
            mod_turns(0, MOD_H // 8)
            pe.wait_ge(par_in, 32)
            for k in range(KT):
                if k == 0:
                    pe.wait_ge(*V0_.at(0, "xn3"))
                if k >= 4:
                    pe.wait_ge(*V0_.at(0, f"xT{k - 4}"))
                for t in range(4):
                    last = nc.tensor.transpose(ps[:, 4 + k % 4, t * P:(t + 1) * P], xs[:, t, k * P:(k + 1) * P], ident)
                last.then_inc(*P0.inc(f"xT{k}"))
            mod_turns(MOD_H // 8, MOD_H // 4)
            pe.wait_ge(*VM.at(MOD_H // 4 - 1, "m1"))
            for i in range(2 * KT):
                last = nc.tensor.transpose(ps[:, 2, 2 * i:2 * i + 2], mrow[0:2, i * P:(i + 1) * P], ident[0:2, 0:2])
            last.then_inc(*PM.inc("rows"))

            with pe.Fori(0, NCH) as j:
                def gate_products(b):
                    pe.wait_ge(*VL.at(j, f"tap{b}3"))
                    pe.wait_ge(*(AL.at(j, "e1_0") if b else AL.at(j - 1, "e1_1")))
                    pe.wait_ge(*(VL.at(j, "iu0") if b else VL.at(j - 1, "iu1")))
                    for d in (0, 1):
                        for w in (0, 1):
                            mm(ps[:, 3 + 2 * w + d, :], wg[:, b, 2 * d + w, :], ub[:, b, :], start=True, stop=True)\
                                .then_inc(*PL.inc(f"g{b}{d}{'ri'[w]}"))

                pe.wait_ge(*AL.at(j - 1, "pad1"))
                for p in range(4):
                    pe.wait_ge(*VH.at(0, f"lo_x{(p + 1) * PIECE - 1}"))
                    proj(LRU0, j, 0, lambda blk, i: (blk, i * T), (hc, hx), part=(p,))
                pe.wait_ge(*VL.at(j - 1, "gl"))
                proj(LRU0, j, 4, lambda blk, i: (2, blk * T), (hx,), part=(0, 1, 2))
                pe.wait_ge(wg_in, j * 16 + 16)
                gate_products(0)
                proj(LRU0, j, 4, lambda blk, i: (2, blk * T), (hx,), part=(3,))
                gate_products(1)

            def chunk_sum(m):
                pe.wait_ge(*VC.at(m, "b"))
                pe.wait_ge(*AC.at(m - 1, "mo"))
                mm(ps[:, 6, 0:CW], ones[:, :], macc[:, :], start=True, stop=True).then_inc(*PC.inc("m"))

            def out_section(n, h0):
                with pe.Fori(0, NCH) as j:
                    pe.wait_ge(*AO[n].at(j - 1, "sg"))
                    proj(h0, j, 0, lambda blk, i: (0, blk * T), (hx,))
                    if n == 0:
                        pe.wait_ge(*VL.at(NCH - 1, "bl1"))
                        pe.wait_ge(*VO[n].at(j - 1, "z"))
                    elif n == 1:
                        pe.wait_ge(*VQ.at(KVH - 1, "al11"))
                        pe.wait_ge(*VO[n].at(j - 1, "z"))
                    else:
                        pe.wait_ge(*VS.at(NCH // 2 - 1, "bl1"))
                        pe.wait_ge(*VO[n].at(j - 1, "z"))
                    proj(h0, j, 4, lambda blk, i: (1, blk * T), (br,))
                    chunk_sum(j + (0, NCH, 3 * NCH)[n])

            out_section(0, OUT0)

            pe.wait_ge(*VO[0].at(NCH - 1, "z"))
            for c in (0, 1):
                proj(KV0, 0, 4 * c, lambda blk, i: (2 * c + blk, i * T), (hc, hx))
            for c in (0, 1):
                tokens(KV0, 0, 0, 8 + 4 * c, lambda t: (ps[:, 4 + 2 * c + t // 2, (t % 2) * CW:(t % 2 + 1) * CW], t % 2 == 0),
                       [(hc, 0), (hc, 1), (hx, 0), (hx, 1)])

            def q_piece(turn, p):
                proj(Q0, turn, p // 4 * 4, lambda blk, i: (p // 4 % 2, blk * T), (hx,), part=(p % 4,))

            def k_ss(h):
                pe.wait_ge(*AK.at(0, f"sq{h}"))
                pe.wait_ge(*VK.at(0, "v3"))
                mm(ps[:, 4 + 2 * (h % 2), :], ones[:, :], nsq[:, :], start=True, stop=True).then_inc(*PK.inc(f"ss{h}"))

            def k_rot(h):
                pe.wait_ge(*VK.at(0, f"kn{h}"))
                mm(ps[:, 5 + 2 * (h % 2), 0:T], rotm, qn[:, T:2 * T], start=True, stop=True).then_inc(*PK.inc(f"rot{h}"))

            def q_ss(u):
                pe.wait_ge(*AN.at(u, "sq"))
                pe.wait_ge(*VN.at(u - 1, "t2"))
                mm(ps[:, 3, :], ones[:, :], nsq[:, :], start=True, stop=True).then_inc(*PN.inc("ss"))

            def q_rot(u):
                pe.wait_ge(*VN.at(u, "qn"))
                mm(ps[:, 3, :], rotm, qn[:, :], start=True, stop=True).then_inc(*PN.inc("rot"))

            k_ss(0)
            k_rot(0)
            q_piece(0, 0)
            k_ss(1)
            q_piece(0, 1)
            q_piece(0, 2)
            k_rot(1)
            k_ss(2)
            q_piece(0, 3)
            q_piece(0, 4)
            k_rot(2)
            k_ss(3)
            q_piece(0, 5)
            q_piece(0, 6)
            k_rot(3)
            q_ss(0)
            q_piece(0, 7)
            q_rot(0)

            def attention_turn(g, more):
                for c in (0, 1):
                    project, norm = more, more or c == 0

                    def score(m):
                        n = 4 * c + m
                        _, hh, qt = units[n]
                        if n >= 3:
                            pe.wait_ge(*AQ.at(g, "ex%d%d%d" % units[n - 3]))
                        mm(ps[:, SB[n % 3], :], qr[:, c, hh * T + qt * P:hh * T + (qt + 1) * P], kS[:, :], start=True, stop=True)\
                            .then_inc(*PQ.inc(f"s{c}{hh}{qt}"))

                    def turned(m):
                        n = 4 * c + m
                        _, hh, qt = units[n]
                        pe.wait_ge(*VQ.at(g, f"pn{c}{hh}{qt}"))
                        pe.wait_ge(*(AQ.at(g, "pt%d%d%d" % units[n - 1]) if n else AQ.at(g - 1, "pt111")))
                        for kt in range(4):
                            last = nc.tensor.transpose(ps[:, 6, kt * P:(kt + 1) * P], pr[:, n % 3, kt * P:(kt + 1) * P], ident)
                        last.then_inc(*PQ.inc(f"t{c}{hh}{qt}"))

                    def weighted(hh):
                        pe.wait_ge(*AQ.at(g, f"pt{c}{hh}1"))
                        pe.wait_ge(staged, 2 * g + 2)
                        pe.wait_ge(*(VQ.at(g, "al%d%d" % divmod(2 * c + hh - 1, 2)) if c or hh else VQ.at(g - 1, "al11")))
                        for kt in range(4):
                            last = mm(ps[:, 7, 0:T], vS[:, kt, :], pT[:, hh, kt, :], start=(kt == 0), stop=(kt == 3))
                        last.then_inc(*PQ.inc(f"o{c}{hh}"))

                    pe.wait_ge(*VN.at(g * 2 + c, "qr"))
                    pe.wait_ge(staged, 2 * g + 1)
                    score(0)
                    score(1)
                    if project:
                        q_piece(g, 8 + 4 * c)
                    if norm:
                        q_ss(g * 2 + (c + 1))
                    score(2)
                    turned(0)
                    if project:
                        q_piece(g, 9 + 4 * c)
                    score(3)
                    turned(1)
                    weighted(0)
                    if project:
                        q_piece(g, 10 + 4 * c)
                    if norm:
                        q_rot(g * 2 + (c + 1))
                    turned(2)
                    if project:
                        q_piece(g, 11 + 4 * c)
                    turned(3)
                    weighted(1)

            with pe.Fori(0, KVH - 1) as g:
                attention_turn(g, True)
            attention_turn(KVH - 1, False)

            pe.wait_ge(*VQ.at(KVH - 1, "al11"))
            out_section(1, OUT1)

            pe.wait_ge(*VO[1].at(NCH - 1, "ya"))
            pe.wait_ge(*AO[1].at(NCH - 1, "sg"))
            with pe.Fori(0, NCH // 2) as i:
                for w in (0, 1):
                    pe.wait_ge(*VS.at(i - 1, f"bg{w}"))
                    for c in range(3):
                        proj(SC0, i, 12 * w + 4 * c, lambda blk, _: (3 * w + c, blk * T), (hx,), per=24)
                    chunk_sum(i * 2 + (2 * NCH + w))

            pe.wait_ge(*AS.at(NCH // 2 - 1, "cg1"))
            out_section(2, OUT2)

            pe.wait_ge(*VO[2].at(NCH - 1, "yl"))
            with pe.Fori(0, NCH // 2) as i:
                for c in (0, 1):
                    pe.wait_ge(*VW.at(i - 1, f"m{c}1"))
                    tokens(WO0, i, 8, 4 * c, lambda t: (ps[:, c, t * CW:(t + 1) * CW], t == 0), [(yf, 0), (yf, 1)])

            for k in range(KT):
                if k in (0, KT // 2):
                    pe.wait_ge(*VF.at(0, f"ha1{k * 2 // KT}"))
                if k >= 4:
                    pe.wait_ge(*AF.at(0, f"hT{k - 4}"))
                for t in (0, 1):
                    last = nc.tensor.transpose(ps[:, 4 + k % 4, t * P:(t + 1) * P], hN[:, t, k * P:(k + 1) * P], ident)
                last.then_inc(*PF.inc(f"hT{k}"))
            pe.wait_ge(*AF.at(0, f"hT{KT - 1}"))

            def route(turn, slot0):
                for q in (0, 1):
                    s = slot0 + q
                    pe.wait_ge(arrived[s], turn * 16 + 16 * (WQ0 // RING + 1))
                    for kk in range(HK):
                        k = q * HK + kk
                        for blk in (0, 1):
                            last = mm(ps[:, 4, blk * T:(blk + 1) * T], W[s][:, kk, blk * P:(blk + 1) * P], hT[:, k, :],
                                      start=(k == 0 and blk == 0), stop=(k == KT - 1), skip_group_check=True)
                    last.then_inc(piece_used, 2)

            def scores(h, first=False):
                pe.wait_ge(*AR.at(h, "q"))
                if not first:
                    pe.wait_ge(*VR.at(h - 1, "ib1_1"))
                pe.wait_ge(keys_in, h * 16 + 16)
                for t in (0, 1):
                    for s in (0, 1):
                        last = mm(ps[:, 5 + t, s * NKEYS:(s + 1) * NKEYS], qT[:, s, t * P:(t + 1) * P], keys[:, s, :],
                                  start=(s == 0), stop=True, skip_group_check=True)
                    last.then_inc(*PR.inc(f"s{t}"))

            def experts(h, *tiles):
                for t in tiles:
                    for k in range(TOPK):
                        n = t * TOPK + k
                        pe.wait_ge(v_in[n % NV], h * (2 * TOPK // NV * 16) + 16 * (n // NV + 1))
                        pe.wait_ge(*AE.at(h, f"dg{t}{k}"))
                        if k == 0:
                            pe.wait_ge(*(VA.at(h, "ac0") if t else VA.at(h - 1, "ac1")))
                        for b in range(4):
                            last = mm(ps[:, b, :], dg[:, k % 4, :], V[n % NV][:, b * 512:(b + 1) * 512],
                                      start=(k == 0), stop=(k == TOPK - 1))
                        last.then_inc(*PE_.inc(f"v{t}{k}"))

            route(0, 0)
            scores(0, True)
            route(0, 2)
            scores(1)
            with pe.Fori(0, PH // 2 - 1) as i:
                for odd in (0, 1):
                    experts(i * 2 + odd, 0)
                    route(i + 1, 2 * odd)
                    scores(i * 2 + (2 + odd))
                    experts(i * 2 + odd, 1)
            experts(PH - 2, 0, 1)
            experts(PH - 1, 0, 1)

        @block.scalar
        def _(act):
            for st_ in PRIMED_A:
                act.sem_inc(st_.sem, st_.ahead)
            fn = nc.scalar.activation
            act.dma_start(par[:, :], a_params).then_inc(par_in, 16)
            act.dma_start(con[:, :], a_consts).then_inc(par_in, 16)
            act.dma_start(xs[:, 0:2, :], a_ctx.rearrange("(t p) d -> p t d", p=P)).then_inc(xs_in, 16)
            act.dma_start(xs[:, 2:4, :], a_x.rearrange("(t p) d -> p t d", p=P)).then_inc(xs_in, 16)
            act.wait_ge(par_in, 32)
            fn(sig0[:, :], pc("c", 0, 2 * KT), ACT.Sigmoid).then_inc(*A0.inc("sig"))
            act.wait_ge(*V0_.at(0, "abs"))
            fn(lm[2][:, :], lm[1][:, :], ACT.Exp, scale=-1.0).then_inc(*A0.inc("ez"))
            act.wait_ge(xs_in, 32)
            for i in range(4):
                if i:
                    act.wait_ge(*A0.at(0, f"ss{i - 1}"))
                fn(junk[:, :], xs[:, i, :], ACT.Square, accum_out=ssq[:, i:i + 1]).then_inc(*A0.inc(f"ss{i}"))
            act.wait_ge(*A0.at(0, "ss3"))
            act.wait_ge(*V0_.at(0, "eps"))
            fn(rin0[:, :], ssq[:, :], ACT.Sqrt, scale=1.0 / D, bias=tiny[:, 1:2]).then_inc(*A0.inc("rt"))

            def split(first, turn, per, p, slots=None):
                s, q = (p // 2) % RING, p % 2
                act.wait_ge(arrived[s], turn * (per * 2) + 16 * ((first + p // 2) // RING + 1))
                act.wait_ge(piece_used, turn * per + (2 * first + p - SPLITS + 1))
                fn(wh[p % SPLITS][:, :, :], W[s][:, q * PIECE:(q + 1) * PIECE, :], ACT.Copy).then_inc(hi_done, 1)

            for k in range(KT):
                for w, to, at in (("c", hc, 0), ("x", hx, T)):
                    act.wait_ge(*VH.at(0, f"{w}{k}"))
                    if k % PIECE == 0 and w == "c":
                        split(LRU0, 0, 0, k // PIECE)
                    fn(to[0][:, k, :], xT[:, k, at:at + T], ACT.Copy).then_inc(*AH.inc(f"{w}{k}"))

            act.wait_ge(*VZ.at(0, "lru"))
            act.dma_start(wg[:, :, :, :], a_gates[0].rearrange("p (b g n) -> p b g n", b=2, g=4)).then_inc(wg_in, 16)
            split(LRU0, 0, 0, AHEAD - 1)
            def lru_turn(j, more):
                def gate_work(b):
                    for d in (0, 1):
                        for w, name in enumerate(("ba", "bx")):
                            act.wait_ge(*PL.at(j, f"g{b}{d}{'ri'[w]}"))
                            fn(ps[:, 3 + 2 * w + d, :], ps[:, 3 + 2 * w + d, :], ACT.Sigmoid,
                               bias=par[:, bass.ds(j * 2 + (PCOLS[name][0] + d * KT + b), 1)]).then_inc(*AL.inc(f"{'ri'[w]}{d}_{b}"))
                    act.wait_ge(*(VL.at(j, "sx0") if b else VL.at(j - 1, "sx1")))
                    act.wait_ge(*AL.at(j, f"i1_{b}"))
                    for d in (0, 1):
                        fn(tt_[:, d, :], ps[:, 3 + d, :], ACT.Tanh, scale=cof[:, 0, bass.ds(j * 2 + (d * KT + b), 1)])\
                            .then_inc(*AL.inc(f"t{d}_{b}"))
                    for d in (0, 1):
                        fn(aa[:, d, :], ps[:, 3 + d, :], ACT.Exp, scale=cof[:, 1, bass.ds(j * 2 + (d * KT + b), 1)])\
                            .then_inc(*AL.inc(f"e{d}_{b}"))
                    act.wait_ge(*AL.at(j, f"t1_{b}"))
                    fn(sq[:, :, :], tt_[:, :, :], ACT.Sqrt, scale=4.0, bias=tiny[:, 0:1]).then_inc(*AL.inc(f"sq{b}"))

                for p in (5, 6, 7):
                    split(LRU0, j, 8, p)
                for b in (0, 1):
                    act.wait_ge(piece_used, j * 8 + (2 * LRU0 + 4))
                    act.wait_ge(*VL.at(j - 1, f"tap{b}3"))
                    fn(pad[:, b, :, LRU_TAPS // 2:LRU_TAPS // 2 + T], ps[:, b, :].rearrange("p (s t) -> p s t", s=2), ACT.Copy)\
                        .then_inc(*AL.inc(f"pad{b}"))
                split(LRU0, j, 8, 8)
                split(LRU0, j, 8, 9)
                split(LRU0, j, 8, 10)
                gate_work(0)
                split(LRU0, j, 8, 11)
                act.wait_ge(piece_used, j * 8 + (2 * LRU0 + 8))
                act.wait_ge(*VL.at(j - 1, "gl"))
                fn(gp[:, :], ps[:, 2, :], ACT.Square).then_inc(*AL.inc("gq"))
                act.wait_ge(*VL.at(j, "gx"))
                fn(gp[:, :], gp[:, :], ACT.Sigmoid, scale=GELU_S).then_inc(*AL.inc("gs"))
                gate_work(1)
                split(LRU0, j, 8, 12)
                if more:
                    act.wait_ge(*PL.at(j, "g11i"))
                    act.dma_start(wg[:, :, :, :], a_gates[bass.ds(j + 1, 1)].rearrange("o p (b g n) -> (o p) b g n", b=2, g=4))\
                        .then_inc(wg_in, 16)

            with act.Fori(0, NCH - 1) as j:
                lru_turn(j, True)
            lru_turn(NCH - 1, False)

            def chunk_load(m, q):
                act.wait_ge(*VC.at(m - 1, "b" if q else f"k{HK - 1}"))
                if q:
                    act.dma_start(brow[0:1, :], a_bmod[bass.ds(m, 1), :]).then_inc(brow_in, 16)
                act.dma_start(mr[q][:, :, :], a_wmod[bass.ds(m * 2 + q, 1)]
                              .rearrange("o p (k n) -> (o p) k n", n=CW)).then_inc(mr_in[q], 16)

            def chunk_store(m):
                act.wait_ge(*PC.at(m, "m"))
                fn(mout[0:1, :], ps[0:1, 6, 0:CW], ACT.Copy).then_inc(*AC.inc("mo"))
                act.wait_ge(*AC.at(m, "mo"))
                act.dma_start(m_flat[bass.ds(m, 1), :], mout[0:1, :]).then_inc(m_stored, 16)

            def out_turn(n, h0, j, more=True):
                m = j + (0, NCH, 3 * NCH)[n]
                for p in (5, 6, 7):
                    split(h0, j, 8, p)
                act.wait_ge(piece_used, j * 8 + (2 * h0 + 4))
                act.wait_ge(*VO[n].at(j - 1, "z"))
                fn((sg if n else sg0)[:, :], ps[:, 0, :], ACT.Sigmoid).then_inc(*AO[n].inc("sg"))
                split(h0, j, 8, 8)
                split(h0, j, 8, 9)
                if more:
                    chunk_load(m + 1, 0)
                split(h0, j, 8, 10)
                split(h0, j, 8, 11)
                if more:
                    chunk_load(m + 1, 1)
                chunk_store(m)
                split(h0, j, 8, 12)
                act.wait_ge(m_stored, m * 16 + 16)

            def out_section(n, h0):
                with act.Fori(0, NCH - (n != 1)) as j:
                    out_turn(n, h0, j)
                if n != 1:
                    out_turn(n, h0, NCH - 1, more=False)

            act.wait_ge(*VL.at(NCH - 1, "bl1"))
            chunk_load(0, 0)
            chunk_load(0, 1)
            out_section(0, OUT0)

            for p in range(5, 20):
                split(KV0, 0, 0, p)
            act.wait_ge(piece_used, 2 * Q0)

            def k_square(h):
                if h:
                    act.wait_ge(*PK.at(0, f"ss{h - 1}"))
                fn(nsq[:, :], ps[:, h, :], ACT.Square).then_inc(*AK.inc(f"sq{h}"))

            def k_root(h):
                act.wait_ge(*PK.at(0, f"ss{h}"))
                if h:
                    act.wait_ge(*VK.at(0, f"kn{h - 1}"))
                fn(nri[:, :], ps[:, 4 + 2 * (h % 2), :], ACT.Sqrt, scale=1.0 / HD, bias=tiny[:, 1:2]).then_inc(*AK.inc(f"rt{h}"))

            def q_square(u, c, used):
                act.wait_ge(piece_used, used)
                act.wait_ge(*PN.at(u - 1, "ss"))
                fn(nsq[:, :], ps[:, c, :], ACT.Square).then_inc(*AN.inc("sq"))

            def q_root(u):
                act.wait_ge(*PN.at(u, "ss"))
                act.wait_ge(*VN.at(u - 1, "qn"))
                fn(nri[:, :], ps[:, 3, :], ACT.Sqrt, scale=1.0 / HD, bias=tiny[:, 1:2]).then_inc(*AN.inc("rt"))

            def stage_keys(g):
                fn(kS[:, :], kT[:, bass.ds(g, 1), :].rearrange("p o t -> p (o t)"), ACT.Copy).then_inc(staged, 1)

            def stage_values(g):
                fn(vS[:, :, :], vT[:, :, bass.ds(g * HD, HD)], ACT.Copy).then_inc(staged, 1)

            k_square(0)
            k_root(0)
            k_square(1)
            k_root(1)
            split(Q0, 0, 0, 4)
            k_square(2)
            split(Q0, 0, 0, 5)
            split(Q0, 0, 0, 6)
            k_root(2)
            k_square(3)
            split(Q0, 0, 0, 7)
            split(Q0, 0, 0, 8)
            k_root(3)
            act.wait_ge(*PK.at(0, "ss3"))
            q_square(0, 0, 2 * Q0 + 4)
            split(Q0, 0, 0, 9)
            split(Q0, 0, 0, 10)
            act.wait_ge(*VK.at(0, "kn3"))
            q_root(0)
            split(Q0, 0, 0, 11)
            act.wait_ge(*VK.at(0, "kr3"))
            stage_keys(0)
            stage_values(0)

            def attention_turn(g, more):
                for c in (0, 1):
                    def ex(m):
                        n = 4 * c + m
                        _, hh, qt = units[n]
                        act.wait_ge(*VQ.at(g, f"nm{c}{hh}{qt}"))
                        act.wait_ge(*(PQ.at(g, "t%d%d%d" % units[n - 3]) if n >= 3 else PQ.at(g - 1, "t111")))
                        fn(pr[:, n % 3, :], ps[:, SB[n % 3], :], ACT.Exp, scale=SCALE, bias=st[:, n, 1:2], accum_out=st[:, n, 2:3])\
                            .then_inc(*AQ.inc(f"ex{c}{hh}{qt}"))

                    def probs(m):
                        _, hh, qt = units[4 * c + m]
                        act.wait_ge(*PQ.at(g, f"t{c}{hh}{qt}"))
                        act.wait_ge(*(PQ.at(g, f"o0{hh}") if c else PQ.at(g - 1, f"o1{hh}")))
                        fn(pT[:, hh, :, qt * P:(qt + 1) * P], ps[:, 6, :].rearrange("p (k t) -> p k t", k=4), ACT.Copy)\
                            .then_inc(*AQ.inc(f"pt{c}{hh}{qt}"))

                    norm = more or c == 0
                    if norm:
                        q_square(g * 2 + (c + 1), 1 - c, g * 8 + (2 * Q0 + 4 * c + 8))
                    ex(0)
                    ex(1)
                    if more:
                        split(Q0, g, 8, 12 + 4 * c)
                    if norm:
                        q_root(g * 2 + (c + 1))
                    ex(2)
                    probs(0)
                    if more:
                        split(Q0, g, 8, 13 + 4 * c)
                    ex(3)
                    if more and c:
                        act.wait_ge(*PQ.at(g, "s111"))
                        stage_keys(g + 1)
                    probs(1)
                    if more:
                        split(Q0, g, 8, 14 + 4 * c)
                    probs(2)
                    if more:
                        split(Q0, g, 8, 15 + 4 * c)
                    probs(3)
                    if more and c:
                        act.wait_ge(*PQ.at(g, "o11"))
                        stage_values(g + 1)

            with act.Fori(0, KVH - 1) as g:
                attention_turn(g, True)
            attention_turn(KVH - 1, False)
            split(OUT1, 0, 0, 4)

            act.wait_ge(*VQ.at(KVH - 1, "al11"))
            chunk_load(NCH, 0)
            chunk_load(NCH, 1)
            out_section(1, OUT1)

            act.wait_ge(*VZ.at(0, "sc"))
            with act.Fori(0, NCH // 2) as i:
                for w in (0, 1):
                    for p in (5, 6, 7):
                        split(SC0, i, 24, 12 * w + p)
                    act.wait_ge(piece_used, i * 24 + (2 * SC0 + 12 * w + 4))
                    act.wait_ge(*(VS.at(i, "cu0") if w else VS.at(i - 1, "cu1")))
                    fn(cg[:, :], ps[:, 3 * w, :], ACT.Copy).then_inc(*AS.inc(f"cg{w}"))
                    m = i * 2 + (2 * NCH + w)
                    for p in range(8, 16):
                        split(SC0, i, 24, 12 * w + p)
                        if p in (11, 13):
                            chunk_load(m + 1, int(p == 13))
                    chunk_store(m)
                    split(SC0, i, 24, 12 * w + 16)
                    act.wait_ge(m_stored, m * 16 + 16)

            out_section(2, OUT2)

            act.wait_ge(piece_used, 2 * WO0)
            act.dma_start(x2[:, :, :], a_x.rearrange("(t p) d -> p t d", p=P)).then_inc(x2_in, 16)
            act.wait_ge(*VO[2].at(NCH - 1, "yl"))
            for i, r in enumerate((m2r, m3r, m4r)):
                act.dma_start(r[:, :], m_dram[i:i + 1, :].to_broadcast([P, D])).then_inc(rows_in, 16)
            act.dma_start(gfr[:, :], a_gffn.to_broadcast([P, D])).then_inc(rows_in, 16)
            with act.Fori(0, NCH // 2 - 1) as i:
                for p in range(5, 13):
                    split(WO0, i, 8, p)
            for p in (5, 6, 7):
                split(WO0, NCH // 2 - 1, 8, p)
            act.wait_ge(*VW.at(NCH // 2 - 1, "a11"))
            for t in (0, 1):
                act.dma_start(x2_dram[t], x2[:, t, :]).then_inc(x2_stored, 16)
            for t in (0, 1):
                if t:
                    act.wait_ge(*AF.at(0, "ss0"))
                fn(junk2[:, :], x2[:, t, :], ACT.Square, accum_out=fst[:, t:t + 1]).then_inc(*AF.inc(f"ss{t}"))
            act.wait_ge(*AF.at(0, "ss1"))
            fn(fst[:, 2:4], fst[:, 0:2], ACT.Sqrt, scale=1.0 / D, bias=tiny[:, 1:2]).then_inc(*AF.inc("rt"))
            act.dma_start(keys[:, :, :], a_keys[0].rearrange("p (s n) -> p s n", s=2)).then_inc(keys_in, 16)
            for k in range(KT):
                act.wait_ge(*PF.at(0, f"hT{k}"))
                fn(hT[:, k, :], ps[:, 4 + k % 4, 0:T], ACT.Copy).then_inc(*AF.inc(f"hT{k}"))
            act.wait_ge(*VF.at(0, "ha11"))
            act.dma_start(m5r[:, :], m_dram[3:4, :].to_broadcast([P, D])).then_inc(last_in, 16)

            def queries(h, first=False):
                act.wait_ge(piece_used, h * 4 + (2 * WQ0 + 4))
                if not first:
                    act.wait_ge(*PR.at(h - 1, "s1"))
                    act.dma_start(keys[:, :, :], a_keys[bass.ds(h, 1)].rearrange("o p (s n) -> (o p) s n", s=2)).then_inc(keys_in, 16)
                fn(qT[:, :, :], ps[:, 4, :].rearrange("p (s t) -> p s t", s=2), ACT.Copy).then_inc(*AR.inc("q"))

            def gates(h, t):
                act.wait_ge(*VR.at(h, f"nm_{t}"))
                fn(gate[:, t, :], ts_[:, :], ACT.Exp, bias=tn[:, 0:1], accum_out=tn[:, 1:2]).then_inc(*AX_.inc(f"ex{t}"))

            def gelus(h, t):
                act.wait_ge(*VE.at(h, f"g3{t}"))
                fn(gw[:, :], gs[:, :], ACT.Sigmoid, scale=GELU_S).then_inc(*AG.inc(f"sg{t}"))

            def diagonals(h, t):
                act.wait_ge(*VE.at(h, f"w{t}"))
                for k in range(TOPK):
                    n = t * TOPK + k
                    act.wait_ge(*(PE_.at(h, "v%d%d" % divmod(n - 4, TOPK)) if n >= 4 else PE_.at(h - 1, f"v1{TOPK - 4 + k}")))
                    fn(dg[:, k % 4, :], ident, ACT.Copy, scale=wt[:, t, k:k + 1]).then_inc(*AE.inc(f"dg{t}{k}"))

            def turn(h, more=True, queries_too=True):
                if more:
                    gates(h + 1, 0)
                diagonals(h, 0)
                gelus(h, 1)
                if more:
                    gates(h + 1, 1)
                if queries_too:
                    queries(h + 2)
                if not more:
                    act.wait_ge(*VE.at(h, "g31"))
                    act.wait_ge(x2_stored, 32)
                    act.dma_start(x2b[:, :, :], x2_dram.rearrange("t p d -> p t d")).then_inc(last_in, 16)
                diagonals(h, 1)
                if more:
                    gelus(h + 1, 0)

            queries(0, True)
            gates(0, 0)
            gates(0, 1)
            queries(1)
            gelus(0, 0)
            with act.Fori(0, PH - 2) as h:
                turn(h)
            turn(PH - 2, queries_too=False)
            turn(PH - 1, more=False, queries_too=False)

        @block.vector
        def _(dve):
            for st_ in PRIMED_V:
                dve.sem_inc(st_.sem, st_.ahead)
            tt, tsc, stt = nc.vector.tensor_tensor, nc.vector.tensor_scalar, nc.vector.scalar_tensor_tensor

            nc.vector.memset(ones[:, :], 1.0).then_inc(*V0_.inc("ones"))
            nc.vector.memset(tiny[:, 0:1], TINY).then_inc(*V0_.inc("tiny"))
            nc.vector.memset(tiny[:, 1:2], EPS).then_inc(*V0_.inc("eps"))
            dve.wait_ge(*A0.at(0, "sig"))
            tt(sT[:, :, :].rearrange("p k v -> p (k v)"), sig0[:, :], pc("c", 0, 2 * KT), ALU.mult).then_inc(*V0_.inc("st"))
            def mod_rows(i0, i1):
                with dve.Fori(i0, i1) as i:
                    for c in (0, 1):
                        dve.wait_ge(piece_used, i * 8 + (4 * c + 4))
                        nc.vector.tensor_copy(mrow[0:2, bass.ds(i * (2 * CW) + c * CW, CW)], ps[0:2, c, 0:CW]).then_inc(*VM.inc(f"m{c}"))

            mod_rows(0, MOD_H // 8 - 1)
            lam = pc("lam", 0, 2 * KT)
            tsc(lm[0][:, :], lam, -1.0, None, ALU.mult).then_inc(*V0_.inc("neg"))
            dve.wait_ge(*V0_.at(0, "neg"))
            tt(lm[1][:, :], lm[0][:, :], lam, ALU.max).then_inc(*V0_.inc("abs"))
            dve.wait_ge(*A0.at(0, "ez"))
            tsc(lm[3][:, :], lm[2][:, :], 2.0, None, ALU.add).then_inc(*V0_.inc("z2"))
            dve.wait_ge(*V0_.at(0, "z2"))
            nc.vector.reciprocal(lm[3][:, :], lm[3][:, :]).then_inc(*V0_.inc("rz"))
            dve.wait_ge(*V0_.at(0, "rz"))
            tt(lm[2][:, :], lm[2][:, :], lm[3][:, :], ALU.mult).then_inc(*V0_.inc("s"))
            dve.wait_ge(*V0_.at(0, "s"))
            tt(lm[3][:, :], lm[2][:, :], lm[2][:, :], ALU.mult).then_inc(*V0_.inc("s2"))
            dve.wait_ge(*V0_.at(0, "s2"))
            tsc(lm[4][:, :], lm[3][:, :], 1.0 / 17, None, ALU.mult).then_inc(*V0_.inc("q0"))
            for i in range(1, 8):
                dve.wait_ge(*V0_.at(0, f"q{i - 1}"))
                stt(lm[4][:, :], lm[4][:, :], 1.0 / (17 - 2 * i), lm[3][:, :], ALU.add, ALU.mult).then_inc(*V0_.inc(f"q{i}"))
            dve.wait_ge(*V0_.at(0, "q7"))
            stt(lm[4][:, :], lm[4][:, :], 1.0, lm[2][:, :], ALU.add, ALU.mult).then_inc(*V0_.inc("s1"))
            tsc(lm[5][:, :], lm[0][:, :], 0.0, None, ALU.max).then_inc(*V0_.inc("mx"))
            dve.wait_ge(*V0_.at(0, "mx"))
            stt(lm[5][:, :], lm[4][:, :], 2.0, lm[5][:, :], ALU.mult, ALU.add).then_inc(*V0_.inc("sp"))
            dve.wait_ge(*V0_.at(0, "sp"))
            tsc(cof[:, 0, :], lm[5][:, :], 4.0, None, ALU.mult).then_inc(*V0_.inc("c4"))
            tsc(cof[:, 1, :], lm[5][:, :], -8.0, None, ALU.mult).then_inc(*V0_.inc("c8"))
            dve.wait_ge(*A0.at(0, "rt"))
            nc.vector.reciprocal(rin0[:, :], rin0[:, :]).then_inc(*V0_.inc("rin"))
            dve.wait_ge(*V0_.at(0, "rin"))
            for i in range(4):
                tsc(xs[:, i, :], xs[:, i, :], rin0[:, i:i + 1], None, ALU.mult).then_inc(*V0_.inc(f"xn{i}"))
            mod_rows(MOD_H // 8 - 1, MOD_H // 8)
            for k in range(KT):
                dve.wait_ge(*P0.at(0, f"xT{k}"))
                nc.vector.tensor_copy(xT[:, k, :], ps[:, 4 + k % 4, :]).then_inc(*V0_.inc(f"xT{k}"))
            mod_rows(MOD_H // 8, MOD_H // 4)
            dve.wait_ge(*PM.at(0, "rows"))
            nc.vector.tensor_copy(mcol[:, :, :], ps[:, 2, 0:4 * KT].rearrange("p (b v) -> p b v", v=2)).then_inc(*VH.inc("col"))
            dve.wait_ge(*VH.at(0, "col"))
            tt(mcol[:, :, :], mcol[:, :, :], pc("b_mod", 0, 2 * KT).unsqueeze(2).to_broadcast([P, 2 * KT, 2]), ALU.add).then_inc(*VH.inc("b"))
            dve.wait_ge(*VH.at(0, "b"))
            stt(mcol[:, KT:2 * KT, :], mcol[:, KT:2 * KT, :], 1.0, pc("norm_mix", 0, KT).unsqueeze(2).to_broadcast([P, KT, 2]),
                ALU.add, ALU.mult).then_inc(*VH.inc("sc"))
            dve.wait_ge(*VH.at(0, "sc"))
            for k in range(KT + LAG):
                if k < KT:
                    tsc(xT[:, k, 0:T], xT[:, k, 0:T], mcol[:, KT + k, 1:2], mcol[:, k, 1:2], ALU.mult, ALU.add).then_inc(*VH.inc(f"c{k}"))
                    tsc(xT[:, k, T:2 * T], xT[:, k, T:2 * T], mcol[:, KT + k, 0:1], mcol[:, k, 0:1], ALU.mult, ALU.add)\
                        .then_inc(*VH.inc(f"x{k}"))
                if k >= LAG:
                    i = k - LAG
                    for w, to, at in (("c", hc, 0), ("x", hx, T)):
                        dve.wait_ge(*AH.at(0, f"{w}{i}"))
                        tt(to[1][:, i, :], xT[:, i, at:at + T], to[0][:, i, :].bitcast(F32), ALU.subtract).then_inc(*VH.inc(f"lo_{w}{i}"))
            dve.wait_ge(*VH.at(0, f"lo_x{KT - 1}"))
            nc.vector.memset(pad[:, :, :, :], 0.0).then_inc(*VZ.inc("lru"))

            with dve.Fori(0, NCH) as j:
                for b in (0, 1):
                    dve.wait_ge(*AL.at(j, f"pad{b}"))
                    dve.wait_ge(*PL.at(j - 1, f"g{b}1i"))
                    uv = ub[:, b, :].rearrange("p (s t) -> p s t", s=2)
                    for k in range(LRU_TAPS):
                        wk = par[:, bass.ds(j * 2 + (PCOLS["lru_w"][0] + k * KT + b), 1)]
                        if k == 0:
                            tsc(uv, pad[:, b, :, 0:T], wk, par[:, bass.ds(j * 2 + (PCOLS["lru_b"][0] + b), 1)],
                                ALU.mult, ALU.add).then_inc(*VL.inc(f"tap{b}0"))
                        else:
                            dve.wait_ge(*VL.at(j, f"tap{b}{k - 1}"))
                            stt(uv, pad[:, b, :, k:k + T], wk, uv, ALU.mult, ALU.add).then_inc(*VL.inc(f"tap{b}{k}"))
                for b in (0, 1):
                    dve.wait_ge(*AL.at(j, f"i1_{b}"))
                    tt(iu[:, :, :], ps[:, 5:7, :], ub[:, b:b + 1, :].to_broadcast([P, 2, 2 * T]), ALU.mult).then_inc(*VL.inc(f"iu{b}"))
                    dve.wait_ge(*AL.at(j, f"e1_{b}"))
                    tsc(aa[:, :, :], aa[:, :, :], 1.0, 0.5, ALU.add, ALU.mult).then_inc(*VL.inc(f"rc{b}"))
                    dve.wait_ge(*AL.at(j, f"sq{b}"))
                    dve.wait_ge(*VL.at(j, f"rc{b}"))
                    stt(tt_[:, :, :], tt_[:, :, :], 1.0, aa[:, :, :], ALU.add, ALU.mult).then_inc(*VL.inc(f"n1{b}"))
                    dve.wait_ge(*VL.at(j, f"n1{b}"))
                    stt(aa[:, :, :], tt_[:, :, :], 2.0, aa[:, :, :], ALU.subtract, ALU.mult).then_inc(*VL.inc(f"n2{b}"))
                    dve.wait_ge(*VL.at(j, f"n2{b}"))
                    tsc(tt_[:, :, :], aa[:, :, :], -2.0, -1.0, ALU.mult, ALU.add).then_inc(*VL.inc(f"a{b}"))
                    tt(sq[:, :, :], sq[:, :, :], aa[:, :, :], ALU.mult).then_inc(*VL.inc(f"dq{b}"))
                    dve.wait_ge(*VL.at(j, f"dq{b}"))
                    tt(iu[:, :, :], iu[:, :, :], sq[:, :, :], ALU.mult).then_inc(*VL.inc(f"dr{b}"))
                    dve.wait_ge(*VL.at(j, f"dr{b}"))
                    scan = nc.vector.tensor_tensor_scan
                    scan(hf[:, :], tt_[:, 0, :], iu[:, 0, :], 0.0, ALU.mult, ALU.add).then_inc(*VL.inc(f"sf{b}"))
                    scan(hb[:, T - 1::-1], tt_[:, 1, T - 1::-1], iu[:, 1, T - 1::-1], 0.0, ALU.mult, ALU.add).then_inc(*VL.inc(f"sc{b}"))
                    dve.wait_ge(*VL.at(j, f"sc{b}"))
                    scan(hb[:, 2 * T - 1:T - 1:-1], tt_[:, 1, 2 * T - 1:T - 1:-1], iu[:, 1, 2 * T - 1:T - 1:-1], hb[:, 0:1],
                         ALU.mult, ALU.add).then_inc(*VL.inc(f"sx{b}"))
                    dve.wait_ge(*VL.at(j, f"sx{b}"))
                    tt(hs[:, :], hf[:, T:2 * T], hb[:, T:2 * T], ALU.add).then_inc(*VL.inc(f"hs{b}"))
                    if b == 0:
                        dve.wait_ge(*AL.at(j, "gq"))
                        tsc(gp[:, :], gp[:, :], GELU_A, 1.0, ALU.mult, ALU.add).then_inc(*VL.inc("gp"))
                        dve.wait_ge(*VL.at(j, "gp"))
                        tt(gp[:, :], gp[:, :], ps[:, 2, :], ALU.mult).then_inc(*VL.inc("gx"))
                        dve.wait_ge(*AL.at(j, "gs"))
                        tt(gl[:, :], gp[:, :], ps[:, 2, :], ALU.mult).then_inc(*VL.inc("gl"))
                    dve.wait_ge(*VL.at(j, "hs1" if b else "gl"))
                    stt(hs[:, :], hs[:, :], -1.0, gl[:, b * T:(b + 1) * T], ALU.mult, ALU.mult).then_inc(*VL.inc(f"ly{b}"))
                    dve.wait_ge(*VL.at(j, f"ly{b}"))
                    row = lambda x: x[:, bass.ds(j * 2 + b, 1), :].rearrange("p o t -> p (o t)")
                    nc.vector.tensor_copy(row(br[0]), hs[:, :]).then_inc(*VL.inc(f"bh{b}"))
                    dve.wait_ge(*VL.at(j, f"bh{b}"))
                    tt(row(br[1]), hs[:, :], row(br[0]).bitcast(F32), ALU.subtract).then_inc(*VL.inc(f"bl{b}"))

            def chunk_products(m):
                dve.wait_ge(*PC.at(m - 1, "m"))
                for k in range(KT):
                    q, kk = divmod(k, HK)
                    if kk == 0:
                        dve.wait_ge(mr_in[q], m * 16 + 16)
                    s = sT[:, k, 0:1]
                    if k == 0:
                        tsc(macc[:, :], mr[q][:, kk, :], s, None, ALU.mult).then_inc(*VC.inc("k0"))
                    else:
                        dve.wait_ge(*VC.at(m, f"k{k - 1}"))
                        stt(macc[:, :], mr[q][:, kk, :], s, macc[:, :], ALU.mult, ALU.add).then_inc(*VC.inc(f"k{k}"))
                dve.wait_ge(brow_in, m * 16 + 16)
                dve.wait_ge(*VC.at(m, f"k{KT - 1}"))
                tt(macc[0:1, :], macc[0:1, :], brow[0:1, :], ALU.add).then_inc(*VC.inc("b"))

            def out_section(n, h0):
                with dve.Fori(0, NCH) as j:
                    chunk_products(j + (0, NCH, 3 * NCH)[n])
                    dve.wait_ge(piece_used, j * 8 + (2 * h0 + 8))
                    dve.wait_ge(*AO[n].at(j, "sg"))
                    yv = y[:, bass.ds(j * 2, 2), :].rearrange("p b t -> p (b t)")
                    if n == 0:
                        tt(yv, ps[:, 1, :], sg0[:, :], ALU.mult).then_inc(*VO[n].inc("z"))
                    else:
                        dve.wait_ge(*VO[n].at(j - 1, "ya"))
                        tt(zt[:, :], ps[:, 1, :], sg[:, :], ALU.mult).then_inc(*VO[n].inc("z"))
                        dve.wait_ge(*VO[n].at(j, "z"))
                        tt(yv, yv, zt[:, :], ALU.add).then_inc(*VO[n].inc("ya"))
                    if n == 2:
                        dve.wait_ge(*VO[n].at(j, "ya"))
                        rows = lambda x: x[:, bass.ds(j * 2, 2), :].rearrange("p b t -> p (b t)")
                        nc.vector.tensor_copy(rows(yf[0]), yv).then_inc(*VO[n].inc("yh"))
                        dve.wait_ge(*VO[n].at(j, "yh"))
                        tt(rows(yf[1]), yv, rows(yf[0]).bitcast(F32), ALU.subtract).then_inc(*VO[n].inc("yl"))

            dve.wait_ge(*VL.at(NCH - 1, "bl1"))
            out_section(0, OUT0)

            dve.wait_ge(piece_used, 2 * Q0)
            dve.wait_ge(*VO[0].at(NCH - 1, "z"))
            for i in range(4):
                nc.vector.tensor_copy(vT[:, (i % 2) * 2:(i % 2) * 2 + 2, (i // 2) * CW:(i // 2 + 1) * CW],
                                      ps[:, 4 + i, :].rearrange("p (t n) -> p t n", t=2)).then_inc(*VK.inc(f"v{i}"))
            for h in range(KVH):
                dve.wait_ge(*AK.at(0, f"rt{h}"))
                nc.vector.reciprocal(nri[:, :], nri[:, :]).then_inc(*VK.inc(f"rc{h}"))
                dve.wait_ge(*VK.at(0, f"rc{h}"))
                stt(qn[:, :], ps[:, h, :], pc("k_norm"), nri[:, :], ALU.mult, ALU.mult).then_inc(*VK.inc(f"kn{h}"))
                dve.wait_ge(*VK.at(0, f"kn{h}"))
                nc.vector.tensor_copy(kT[:, h, 0:T], qn[:, 0:T]).then_inc(*VK.inc(f"kc{h}"))
                tt(rt1[:, 0:T], qn[:, T:2 * T], cosT, ALU.mult).then_inc(*VK.inc(f"t1{h}"))
                dve.wait_ge(*PK.at(0, f"rot{h}"))
                tt(rt2[:, 0:T], ps[:, 5 + 2 * (h % 2), 0:T], sinT, ALU.mult).then_inc(*VK.inc(f"t2{h}"))
                dve.wait_ge(*VK.at(0, f"t2{h}"))
                tt(kT[:, h, T:2 * T], rt1[:, 0:T], rt2[:, 0:T], ALU.add).then_inc(*VK.inc(f"kr{h}"))

            two = lambda x: x.rearrange("p (h t) -> p h t", h=2)

            def q_norm(u, c):
                dve.wait_ge(*AN.at(u, "rt"))
                nc.vector.reciprocal(nri[:, :], nri[:, :]).then_inc(*VN.inc("rc"))
                dve.wait_ge(*VN.at(u, "rc"))
                dve.wait_ge(*PN.at(u - 1, "rot"))
                stt(qn[:, :], ps[:, c, :], pc("q_norm"), nri[:, :], ALU.mult, ALU.mult).then_inc(*VN.inc("qn"))
                dve.wait_ge(*VN.at(u, "qn"))
                tt(two(rt1[:, :]), two(qn[:, :]), cosT.unsqueeze(1).to_broadcast([P, 2, T]), ALU.mult).then_inc(*VN.inc("t1"))

            def q_rotation(g, u, c):
                dve.wait_ge(*PN.at(u, "rot"))
                tt(two(rt2[:, :]), two(ps[:, 3, :]), sinT.unsqueeze(1).to_broadcast([P, 2, T]), ALU.mult).then_inc(*VN.inc("t2"))
                dve.wait_ge(*VN.at(u, "t2"))
                dve.wait_ge(*PQ.at(g, f"s{c}11"))
                tt(qr[:, c, :], rt1[:, :], rt2[:, :], ALU.add).then_inc(*VN.inc("qr"))

            dve.wait_ge(*VK.at(0, "kr3"))
            q_norm(0, 0)
            q_rotation(-1, 0, 0)

            def attention_turn(g, more):
                for c in (0, 1):
                    def peak(m):
                        n = 4 * c + m
                        u = "%d%d%d" % units[n]
                        dve.wait_ge(*PQ.at(g, "s" + u))
                        nc.vector.reduce_max(st[:, n, 0:1], ps[:, SB[n % 3], :], AX.X).then_inc(*VQ.inc("mx" + u))
                        dve.wait_ge(*VQ.at(g, "mx" + u))
                        tsc(st[:, n, 1:2], st[:, n, 0:1], -SCALE, None, ALU.mult).then_inc(*VQ.inc("nm" + u))

                    def normed(m):
                        n = 4 * c + m
                        u = "%d%d%d" % units[n]
                        dve.wait_ge(*AQ.at(g, "ex" + u))
                        nc.vector.reciprocal(st[:, n, 3:4], st[:, n, 2:3]).then_inc(*VQ.inc("rs" + u))
                        dve.wait_ge(*VQ.at(g, "rs" + u))
                        tsc(pr[:, n % 3, :], pr[:, n % 3, :], st[:, n, 3:4], None, ALU.mult).then_inc(*VQ.inc("pn" + u))

                    def head_out(hh):
                        dve.wait_ge(*PQ.at(g, f"o{c}{hh}"))
                        row = lambda x: x[:, bass.ds(g * 4 + (2 * c + hh), 1), :].rearrange("p o t -> p (o t)")
                        nc.vector.tensor_copy(row(br[0]), ps[:, 7, 0:T]).then_inc(*VQ.inc(f"av{c}{hh}"))
                        dve.wait_ge(*VQ.at(g, f"av{c}{hh}"))
                        tt(row(br[1]), ps[:, 7, 0:T], row(br[0]).bitcast(F32), ALU.subtract).then_inc(*VQ.inc(f"al{c}{hh}"))

                    norm = more or c == 0
                    peak(0)
                    peak(1)
                    normed(0)
                    peak(2)
                    normed(1)
                    peak(3)
                    if norm:
                        q_norm(g * 2 + (c + 1), 1 - c)
                    normed(2)
                    head_out(0)
                    if norm:
                        q_rotation(g if c else g - 1, g * 2 + (c + 1), 1 - c)
                    normed(3)
                    head_out(1)

            with dve.Fori(0, KVH - 1) as g:
                attention_turn(g, True)
            attention_turn(KVH - 1, False)

            dve.wait_ge(*VQ.at(KVH - 1, "al11"))
            out_section(1, OUT1)

            dve.wait_ge(*VO[1].at(NCH - 1, "ya"))
            nc.vector.memset(cu[:, :, :], 0.0).then_inc(*VZ.inc("sc"))
            dve.wait_ge(*VZ.at(0, "sc"))
            with dve.Fori(0, NCH // 2) as i:
                for w in (0, 1):
                    chunk_products(i * 2 + (2 * NCH + w))
                    dve.wait_ge(piece_used, i * 24 + (2 * SC0 + 12 * w + 8))
                    dve.wait_ge(*AS.at(i, f"cg{w}"))
                    two = lambda x: x.rearrange("p (b t) -> p b t", b=2)
                    tt(cu[:, :, 1:1 + T], two(cg[:, :]), two(ps[:, 3 * w + 1, :]), ALU.mult).then_inc(*VS.inc(f"cu{w}"))
                    dve.wait_ge(*VS.at(i, f"cu{w}"))
                    for k in range(SC_TAPS):
                        if k:
                            dve.wait_ge(*VS.at(i, f"k{k - 1}1_{w}"))
                        for b in (0, 1):
                            wk = par[:, bass.ds(i * 4 + (PCOLS["sc_w"][0] + k * KT + 2 * w + b), 1)]
                            if k == 0:
                                tsc(cv[:, b, :], cu[:, b, 0:T], wk, par[:, bass.ds(i * 4 + (PCOLS["sc_b"][0] + 2 * w + b), 1)],
                                    ALU.mult, ALU.add).then_inc(*VS.inc(f"k0{b}_{w}"))
                            else:
                                stt(cv[:, b, :], cu[:, b, k:k + T], wk, cv[:, b, :], ALU.mult, ALU.add).then_inc(*VS.inc(f"k{k}{b}_{w}"))
                    dve.wait_ge(piece_used, i * 24 + (2 * SC0 + 12 * w + 12))
                    dve.wait_ge(*VS.at(i, f"k21_{w}"))
                    tt(cb[:, :], cv[:, :, :].rearrange("p b t -> p (b t)"), ps[:, 3 * w + 2, :], ALU.mult).then_inc(*VS.inc(f"bg{w}"))
                    dve.wait_ge(*VS.at(i, f"bg{w}"))
                    rows = lambda x: x[:, bass.ds(i * 4 + 2 * w, 2), :].rearrange("p b t -> p (b t)")
                    nc.vector.tensor_copy(rows(br[0]), cb[:, :]).then_inc(*VS.inc(f"bh{w}"))
                    dve.wait_ge(*VS.at(i, f"bh{w}"))
                    tt(rows(br[1]), cb[:, :], rows(br[0]).bitcast(F32), ALU.subtract).then_inc(*VS.inc(f"bl{w}"))

            dve.wait_ge(*VS.at(NCH // 2 - 1, "bl1"))
            out_section(2, OUT2)

            dve.wait_ge(*VO[2].at(NCH - 1, "ya"))
            dve.wait_ge(x2_in, 16)
            dve.wait_ge(rows_in, 64)
            with dve.Fori(0, NCH // 2) as i:
                for c in (0, 1):
                    dve.wait_ge(piece_used, i * 8 + (2 * WO0 + 4 * c + 4))
                    for t in (0, 1):
                        dve.wait_ge(*(VW.at(i, f"a{c}0") if t else (VW.at(i, "a01") if c else VW.at(i - 1, "a11"))))
                        tt(xm[:, :], ps[:, c, t * CW:(t + 1) * CW], m2r[:, bass.ds(i * 512 + c * CW, CW)], ALU.mult).then_inc(*VW.inc(f"m{c}{t}"))
                        dve.wait_ge(*VW.at(i, f"m{c}{t}"))
                        xv = x2[:, t, bass.ds(i * 512 + c * CW, CW)]
                        tt(xv, xv, xm[:, :], ALU.add).then_inc(*VW.inc(f"a{c}{t}"))
            stt(gfr[:, :], m4r[:, :], 1.0, gfr[:, :], ALU.add, ALU.mult).then_inc(*VF.inc("g1"))
            dve.wait_ge(*AF.at(0, "rt"))
            nc.vector.reciprocal(fst[:, 4:6], fst[:, 2:4]).then_inc(*VF.inc("rc0"))
            dve.wait_ge(*VF.at(0, "rc0"))
            for half in (0, 1):
                cols_ = slice(half * D // 2, (half + 1) * D // 2)
                for t in (0, 1):
                    stt(hN[:, t, cols_], x2[:, t, cols_], fst[:, 4 + t:5 + t], gfr[:, cols_], ALU.mult, ALU.mult).then_inc(*VF.inc(f"hm{t}{half}"))
                    dve.wait_ge(*VF.at(0, f"hm{t}{half}"))
                    tt(hN[:, t, cols_], hN[:, t, cols_], m3r[:, cols_], ALU.add).then_inc(*VF.inc(f"ha{t}{half}"))
            nc.vector.memset(acc[:, :, :], 0.0).then_inc(*VF.inc("acc0"))
            dve.wait_ge(*VF.at(0, "acc0"))

            def route(h, t, odd, used=True):
                dve.wait_ge(*PR.at(h, f"s{t}"))
                n = lambda x: x + f"_{t}"

                def top8s(src, copy, vals, inds, names):
                    ma, ia, mr_, mb, ib = (n(x) for x in names)
                    apart(dve)
                    nc.vector.max(vals[:, 0:8], src).then_inc(*VR.inc(ma))
                    dve.wait_ge(*VR.at(h, ma))
                    apart(dve)
                    nc.vector.max_index(inds[:, 0:8], vals[:, 0:8], src).then_inc(*VR.inc(ia))
                    nc.vector.match_replace(copy, vals[:, 0:8], src, LOW).then_inc(*VR.inc(mr_))
                    dve.wait_ge(*VR.at(h, mr_))
                    apart(dve)
                    nc.vector.max(vals[:, 8:16], copy).then_inc(*VR.inc(mb))
                    dve.wait_ge(*VR.at(h, mb))
                    apart(dve)
                    nc.vector.max_index(inds[:, 8:16], vals[:, 8:16], copy).then_inc(*VR.inc(ib))

                for s in (0, 1):
                    top8s(ps[:, 5 + t, s * NKEYS:(s + 1) * NKEYS], rep[:, s * NKEYS:(s + 1) * NKEYS], tv[:, s, :], ti[:, s, :],
                          [f"{w}{s}" for w in ("ma", "ia", "mr", "mb", "ib")])
                dve.wait_ge(*VR.at(h, n("ib1")))
                sq_ = [P, TOPK, TOPK]
                tt(cand[:, :, :], tv[:, 0, :].unsqueeze(2).to_broadcast(sq_), tv[:, 1, :].unsqueeze(1).to_broadcast(sq_), ALU.add)\
                    .then_inc(*VR.inc(n("cand")))
                dve.wait_ge(*VR.at(h, n("cand")))
                flat = lambda x: x[:, :, :].rearrange("p a b -> p (a b)")
                top8s(flat(cand), flat(crep), ts_, tp, ("ma2", "ia2", "mr2", "mb2", "ib2"))
                nc.vector.tensor_copy(tif[:, :, :], ti[:, :, :]).then_inc(*VR.inc(n("fi")))
                dve.wait_ge(*VR.at(h, n("fi")))
                tsc(tph[:, 0, :], tp[:, :], 4, None, ALU.logical_shift_right).then_inc(*VR.inc(n("hi")))
                tsc(tph[:, 1, :], tp[:, :], TOPK - 1, None, ALU.bitwise_and).then_inc(*VR.inc(n("lo")))
                dve.wait_ge(*VR.at(h, n("lo")))
                nc.vector.tensor_copy(tpf[:, :, :], tph[:, :, :]).then_inc(*VR.inc(n("fp")))
                dve.wait_ge(*VR.at(h, n("fp")))
                for s in (0, 1):
                    tt(oh[:, :, :], tpf[:, s, :].unsqueeze(2).to_broadcast(sq_), iota.unsqueeze(1).to_broadcast(sq_), ALU.is_equal)\
                        .then_inc(*VR.inc(n(f"o{s + 1}")))
                    dve.wait_ge(*VR.at(h, n(f"o{s + 1}")))
                    tt(oh[:, :, :], oh[:, :, :], tif[:, s, :].unsqueeze(1).to_broadcast(sq_), ALU.mult).then_inc(*VR.inc(n(f"p{s + 1}")))
                    dve.wait_ge(*VR.at(h, n(f"p{s + 1}")))
                    nc.vector.reduce_sum(te[:, s, :], oh[:, :, :], AX.X).then_inc(*VR.inc(n(f"e{s + 1}")))
                    dve.wait_ge(*VR.at(h, n(f"e{s + 1}")))
                tsc(tn[:, 0:1], ts_[:, 0:1], -1.0, None, ALU.mult).then_inc(*VR.inc(n("nm")))
                dve.wait_ge(*AX_.at(h, f"ex{t}"))
                nc.vector.reciprocal(tn[:, 2:3], tn[:, 1:2]).then_inc(*VR.inc(n("rg")))
                dve.wait_ge(*VR.at(h, n("rg")))
                tsc(gate[:, t, :], gate[:, t, :], tn[:, 2:3], None, ALU.mult).then_inc(*VR.inc(n("gt")))
                if used:
                    dve.wait_ge(*PE_.at(h - 2, f"v{t}{TOPK - 1}"))
                stt(idx[:, odd, t, :], te[:, 0, :], float(NKEYS), te[:, 1, :], ALU.mult, ALU.add).then_inc(*VR.inc(n("idx")))

            def dots(h, t):
                for k in range(TOPK):
                    n = t * TOPK + k
                    dve.wait_ge(u_in[n % NU], h * (2 * TOPK // NU * 16) + 16 * (n // NU + 1))
                    stt(U[n % NU][:, :], U[n % NU][:, :], 1.0, hN[:, t, :], ALU.mult, ALU.mult, accum_out=dot[:, t, k:k + 1])\
                        .then_inc(*VE.inc(f"d{t}{k}"))
                dve.wait_ge(*VE.at(h, f"d{t}{TOPK - 1}"))
                tt(gs[:, :], dot[:, t, :], dot[:, t, :], ALU.mult).then_inc(*VE.inc(f"g1{t}"))
                dve.wait_ge(*VE.at(h, f"g1{t}"))
                tsc(gs[:, :], gs[:, :], GELU_A, 1.0, ALU.mult, ALU.add).then_inc(*VE.inc(f"g2{t}"))
                dve.wait_ge(*VE.at(h, f"g2{t}"))
                tt(gs[:, :], gs[:, :], dot[:, t, :], ALU.mult).then_inc(*VE.inc(f"g3{t}"))
                dve.wait_ge(*AG.at(h, f"sg{t}"))
                tt(gw[:, :], gw[:, :], dot[:, t, :], ALU.mult).then_inc(*VE.inc(f"g4{t}"))
                dve.wait_ge(*VE.at(h, f"g4{t}"))
                dve.wait_ge(*AE.at(h - 1, f"dg{t}{TOPK - 1}"))
                tt(wt[:, t, :], gw[:, :], gate[:, t, :], ALU.mult).then_inc(*VE.inc(f"w{t}"))

            def add(h, t):
                dve.wait_ge(*PE_.at(h, f"v{t}{TOPK - 1}"))
                tt(acc[:, t, :], acc[:, t, :], ps[:, 0:4, :].rearrange("p b n -> p (b n)"), ALU.add).then_inc(*VA.inc(f"ac{t}"))

            def turn(h, odd, more=True, used=True):
                if more:
                    route(h + 1, 0, 1 - odd, used)
                dots(h, 1)
                add(h, 0)
                if more:
                    route(h + 1, 1, 1 - odd, used)
                    dots(h + 1, 0)
                else:
                    final(0)
                add(h, 1)

            def final(t):
                dve.wait_ge(*VA.at(PH - 1, f"ac{t}"))
                dve.wait_ge(last_in, 32)
                tt(acc[:, t, :], acc[:, t, :], m5r[:, :], ALU.mult).then_inc(*VX.inc(f"m{t}"))
                dve.wait_ge(*VX.at(0, f"m{t}"))
                tt(acc[:, t, :], acc[:, t, :], x2b[:, t, :], ALU.add).then_inc(*VX.inc(f"o{t}"))

            route(0, 0, 0, False)
            dve.wait_ge(*VR.at(0, "idx_0"))
            route(0, 1, 0, False)
            dve.wait_ge(*VR.at(0, "idx_1"))
            dots(0, 0)
            turn(0, 0, used=False)
            with dve.Fori(0, PH // 2 - 1) as i:
                turn(i * 2 + 1, 1)
                turn(i * 2 + 2, 0)
            turn(PH - 1, 1, more=False)
            final(1)

        @block.gpsimd
        def _(pool):
            sub = lambda out_, a, b: nc.gpsimd.tensor_tensor(out_, a, b, ALU.subtract)
            with pool.Fori(0, (WQ0 - LRU0) // RING) as i:
                for p in range(2 * RING):
                    pool.wait_ge(hi_done, i * (2 * RING) + p + 1)
                    sub(wl[p % SPLITS][:, :, :], W[p // 2][:, (p % 2) * PIECE:(p % 2 + 1) * PIECE, :], wh[p % SPLITS][:, :, :].bitcast(F32))\
                        .then_inc(lo_done, 1)

            def rows_u(h, odd, t, k):
                n = t * TOPK + k
                if k == 0:
                    pool.wait_ge(*VR.at(h, f"idx_{t}"))
                pool.wait_ge(*(VE.at(h, "d%d%d" % divmod(n - NU, TOPK)) if n >= NU else VE.at(h - 1, f"d1{TOPK - NU + k}")))
                apart(pool)
                nc.gpsimd.indirect_dma_start(out=U[n % NU][:, :], out_offset=None, in_=a_u,
                                             in_offset=bass.IndirectOffsetOnAxis(ap=idx[:, odd, t, k:k + 1], axis=0)).then_inc(u_in[n % NU], 16)

            def rows_v(h, odd, t, k):
                n = t * TOPK + k
                pool.wait_ge(*(PE_.at(h, "v%d%d" % divmod(n - NV, TOPK)) if n >= NV else PE_.at(h - 1, f"v1{TOPK - NV + k}")))
                apart(pool)
                nc.gpsimd.indirect_dma_start(out=V[n % NV][:, :], out_offset=None, in_=a_v,
                                             in_offset=bass.IndirectOffsetOnAxis(ap=idx[:, odd, t, k:k + 1], axis=0)).then_inc(v_in[n % NV], 16)

            def turn(h, odd, more=True, begun=0):
                for k in range(TOPK):
                    rows_u(h, odd, 1, k)
                    if k + begun < TOPK:
                        rows_v(h, odd, 0, k + begun)
                for k in range(TOPK):
                    if more:
                        rows_u(h + 1, 1 - odd, 0, k)
                    rows_v(h, odd, 1, k)

            pool.wait_ge(*VF.at(0, "ha11"))
            for k in range(TOPK):
                rows_u(0, 0, 0, k)
                if k == NU - 1:
                    pool.wait_ge(x2_stored, 32)
                    for kv in range(4):
                        rows_v(0, 0, 0, kv)
            turn(0, 0, begun=4)
            with pool.Fori(0, PH // 2 - 1) as i:
                turn(i * 2 + 1, 1)
                turn(i * 2 + 2, 0)
            turn(PH - 1, 1, more=False)


def kernel(**inputs):
    import concourse.bacc as bacc
    from concourse.bass_utils import run_bass_kernel_spmd as run

    a = {k: np.asarray(v) for k, v in inputs.items()}

    def cols(v):
        v = v.reshape(-1, KT, P)
        return v.transpose(2, 0, 1).reshape(P, -1)

    def halves(w):
        n = w.shape[1] // CW
        return w.reshape(2, HK, P, n, CW).transpose(3, 0, 2, 1, 4).reshape(2 * n, P, HK * CW)

    w_mod, w_in = halves(a["w_mod"][0]), halves(a["w_in"][0])
    q, k, v, lx, lg, bg, cg, u, g0, g1, g2 = (int(x) // CW * 2 for x in np.cumsum(
        [0, D, KVH * HD, KVH * HD] + [D] * 7))
    take = lambda at, n=NCH: w_in[at:at + 2 * n].reshape(n, 2, P, HK * CW)
    chunks = lambda w: halves(w).reshape(NCH, 2, P, HK * CW)
    mix = lambda *parts: np.stack(parts, axis=1).reshape(-1, P, HK * CW)
    stream = np.concatenate([
        w_mod[:MOD_H], mix(take(lx), take(lg)), mix(take(g1), chunks(a["w_o_lru"][0])),
        w_in[k:k + 4], w_in[v:v + 4], w_in[q:q + 2 * NCH], mix(take(g0), chunks(a["w_o_attn"][0])),
        mix(take(cg), take(u), take(bg)), mix(take(g2), chunks(a["w_o_sc"][0])),
        halves(a["w_out"][0]), halves(a["peer_wq"][0])])
    assert len(stream) == HALVES

    cc = np.stack([cols(a["c"])[:, :], cols(a["c_ctx"])], axis=2).reshape(P, 2 * KT)
    params = np.concatenate([
        cc, cols(a["b_mod"][0, :2 * D]), cols(a["norm_mix"]), a["q_norm"].reshape(P, 1), a["k_norm"].reshape(P, 1),
        cols(a["lru_conv_w"][0]), cols(a["lru_conv_b"]), cols(a["lru_ba"][0]), cols(a["lru_bx"][0]), cols(a["lru_lambda"][0]),
        cols(a["sc_conv_w"][0]), cols(a["sc_conv_b"])], axis=1)
    gates = np.stack([a["lru_wa"][0], a["lru_wx"][0]], axis=1)
    gates = gates.reshape(2, 2, NCH, 2, P, P).transpose(2, 4, 3, 0, 1, 5).reshape(NCH, P, -1)
    keys = np.stack([a["peer_k1"][0], a["peer_k2"][0]], axis=1).transpose(0, 3, 1, 2).reshape(PH, P, 2 * NKEYS)

    inv = (10000.0 ** (-np.arange(ROPE_PAIRS, dtype=np.float32) / ROPE_PAIRS)).astype(np.float32)
    pos = np.arange(T)
    row, col = (pos // GRID_W).astype(np.float32), (pos % GRID_W).astype(np.float32)
    angle = np.concatenate([row[:, None] * inv, row[:, None] * inv, col[:, None] * inv, col[:, None] * inv], axis=1).T
    rot = np.zeros((P, P), np.float32)
    for base in (0, 2 * ROPE_PAIRS):
        for i in range(ROPE_PAIRS):
            rot[base + ROPE_PAIRS + i, base + i] = -1.0
            rot[base + i, base + ROPE_PAIRS + i] = 1.0
    consts = np.concatenate([np.eye(P), rot, np.cos(angle.astype(np.float64)), np.sin(angle.astype(np.float64)),
                             np.tile(np.arange(TOPK), (P, 1))], axis=1).astype(np.float32)

    arrays = {
        "stream": stream, "params": params, "consts": consts, "x": a["x"][0], "ctx": a["ctx"][0], "gates": gates,
        "wmod": w_mod[MOD_H:], "bmod": a["b_mod"][0, 2 * D:].reshape(4 * NCH, CW), "gffn": a["norm_ffn"], "keys": keys,
        "peer_u": a["peer_u"][0], "peer_v": a["peer_v"][0],
    }
    nc = bacc.Bacc("TRN2", target_bir_lowering=False, num_devices=1)
    args = []
    for name, x in arrays.items():
        arrays[name] = x = np.ascontiguousarray(x)
        args.append(nc.dram_tensor(f"in_{name}", x.shape, mybir.dt.from_np(x.dtype), kind="ExternalInput").ap())
    args.append(nc.dram_tensor("out", (2, P, D), F32, kind="ExternalOutput").ap())
    build(nc, *args)
    r = run(nc, [{f"in_{k}": v for k, v in arrays.items()}], core_ids=[0])
    return r.results[0]["out"].reshape(1, 2 * P, D)
```
